# Optimizing a Trainium2 kernel written in Bass

```python
import functools
import jax, jax.numpy as jnp
from jax import lax
import numpy as np

D_MODEL = 1024
BATCH = 1
SEQ = 1024
DEPTH = 1
DEC_BATCH = 8
DEC_SEQ = 4
PAST_LEN = 4096
PAGE_SIZE = 128

N_HEADS = 8
HEAD_DIM = 64
ATT_WIDTH = N_HEADS * HEAD_DIM
Q_BLOCK = 128
CONV_CH = D_MODEL // 2
CONV_WIDTH = 31
PEER_HEADS = 8
N_KEYS = 128
N_EXPERTS = N_KEYS * N_KEYS
PEER_KEY_DIM = 256
HALF_KEY = PEER_KEY_DIM // 2
TOPK = 16
PEER_BLOCK = 128
PLE_DIM = 256
RMS_EPS = 1e-6
LN_EPS = 1e-5
IN_SPLITS = (ATT_WIDTH, 2 * ATT_WIDTH, 3 * ATT_WIDTH, 3 * ATT_WIDTH + N_HEADS,
             3 * ATT_WIDTH + N_HEADS + CONV_CH, 3 * ATT_WIDTH + N_HEADS + 2 * CONV_CH,
             3 * ATT_WIDTH + N_HEADS + 2 * CONV_CH + D_MODEL)
IN_COLS = 3 * ATT_WIDTH + N_HEADS + 2 * CONV_CH + 2 * D_MODEL

kernel_name = 'fox_conformer_peer_hybrid_step'

F32 = jnp.float32

def rmsnorm(x, g):
    xf = x.astype(F32)
    y = xf * lax.rsqrt(jnp.mean(xf * xf, axis=-1, keepdims=True) + RMS_EPS)
    return (y * g.astype(F32)).astype(x.dtype)

def layernorm(x, g, b):
    xf = x.astype(F32)
    mu = jnp.mean(xf, axis=-1, keepdims=True)
    var = jnp.mean(jnp.square(xf - mu), axis=-1, keepdims=True)
    y = (xf - mu) * lax.rsqrt(var + LN_EPS)
    return (y * g.astype(F32) + b.astype(F32)).astype(x.dtype)

def in_projection(h, g_mix, w_in, b_f):
    u = rmsnorm(h, g_mix)
    z = u @ w_in
    q, k, v, fl, ca, cb, ga, gc = jnp.split(z, IN_SPLITS, axis=-1)
    lead = h.shape[:-1]
    q = q.reshape(*lead, N_HEADS, HEAD_DIM)
    k = k.reshape(*lead, N_HEADS, HEAD_DIM)
    v = v.reshape(*lead, N_HEADS, HEAD_DIM)
    logf = jax.nn.log_sigmoid(fl.astype(F32) + b_f.astype(F32))
    glu = ca * jax.nn.sigmoid(cb)
    return q, k, v, logf, glu, ga, gc

def fox_prompt(q, k, v, logf):
    B, S, H, Dh = q.shape
    scale = HEAD_DIM ** -0.5
    cum = jnp.cumsum(logf, axis=1)
    nb = S // Q_BLOCK
    qb = jnp.swapaxes(q.reshape(B, nb, Q_BLOCK, H, Dh), 0, 1)
    cqb = jnp.swapaxes(cum.reshape(B, nb, Q_BLOCK, H), 0, 1)
    qpos = jnp.arange(S, dtype=jnp.int32).reshape(nb, Q_BLOCK)
    kpos = jnp.arange(S, dtype=jnp.int32)
    cum_k = jnp.swapaxes(cum, 1, 2)

    def block(args):
        qi, ci, pi = args
        s = jnp.einsum('bqhd,bkhd->bhqk', qi, k).astype(F32) * scale
        s = s + jnp.swapaxes(ci, 1, 2)[..., None] - cum_k[:, :, None, :]
        s = jnp.where(kpos[None, None, None, :] <= pi[None, None, :, None], s, -jnp.inf)
        p = jax.nn.softmax(s, axis=-1).astype(v.dtype)
        return jnp.einsum('bhqk,bkhd->bqhd', p, v)

    o = lax.map(block, (qb, cqb, qpos))
    return jnp.swapaxes(o, 0, 1).reshape(B, S, H * Dh)

def fox_sample(q, k, v, logf, cache_k, cache_v, cache_lf, page_table):
    Bd, Sd, H, Dh = q.shape
    scale = HEAD_DIM ** -0.5
    L = page_table.shape[1] * cache_k.shape[1]
    kp = cache_k[page_table].reshape(Bd, L, H, Dh)
    vp = cache_v[page_table].reshape(Bd, L, H, Dh)
    lfp = cache_lf[page_table].reshape(Bd, L, H).astype(F32)
    excl = lax.cumsum(lfp, axis=1, reverse=True) - lfp
    cnew_t = jnp.swapaxes(jnp.cumsum(logf, axis=1), 1, 2)
    s_past = jnp.einsum('bqhd,bkhd->bhqk', q, kp).astype(F32) * scale
    s_past = s_past + jnp.swapaxes(excl, 1, 2)[:, :, None, :] + cnew_t[..., :, None]
    s_new = jnp.einsum('bqhd,bkhd->bhqk', q, k).astype(F32) * scale
    s_new = s_new + cnew_t[..., :, None] - cnew_t[..., None, :]
    causal = jnp.arange(Sd)[None, :] <= jnp.arange(Sd)[:, None]
    s_new = jnp.where(causal, s_new, -jnp.inf)
    p = jax.nn.softmax(jnp.concatenate([s_past, s_new], axis=-1), axis=-1).astype(v.dtype)
    o = (jnp.einsum('bhqk,bkhd->bqhd', p[..., :L], vp)
         + jnp.einsum('bhqk,bkhd->bqhd', p[..., L:], v))
    return o.reshape(Bd, Sd, H * Dh)

def conv_branch(glu_ext, w_dw, b_dw, ln_g, ln_b, w_conv_proj):
    y = lax.conv_general_dilated(
        glu_ext, w_dw[:, None, :].astype(glu_ext.dtype), window_strides=(1,), padding='VALID',
        dimension_numbers=('NWC', 'WIO', 'NWC'), feature_group_count=CONV_CH)
    y = jax.nn.silu(layernorm(y + b_dw, ln_g, ln_b))
    return y @ w_conv_proj

def peer(u, w_pq, sub_keys, exp_u, exp_v):
    lead = u.shape[:-1]
    x = u.reshape(-1, D_MODEL)
    T = x.shape[0]
    nb = -(-T // PEER_BLOCK)
    x = jnp.pad(x, ((0, nb * PEER_BLOCK - T), (0, 0))).reshape(nb, PEER_BLOCK, D_MODEL)

    def block(xb):
        q = (xb @ w_pq).reshape(PEER_BLOCK, PEER_HEADS, 2, HALF_KEY)
        s = jnp.einsum('thpd,pnd->thpn', q, sub_keys).astype(F32)
        sv, si = lax.top_k(s, TOPK)
        comb = (sv[:, :, 0, :, None] + sv[:, :, 1, None, :]).reshape(PEER_BLOCK, PEER_HEADS, TOPK * TOPK)
        cidx = (si[:, :, 0, :, None] * N_KEYS + si[:, :, 1, None, :]).reshape(PEER_BLOCK, PEER_HEADS, TOPK * TOPK)
        tv, ti = lax.top_k(comb, TOPK)
        eidx = jnp.take_along_axis(cidx, ti, axis=-1)
        g = jax.nn.softmax(tv, axis=-1)
        ue = exp_u[eidx]
        ve = exp_v[eidx]
        a = jax.nn.gelu(jnp.einsum('td,thkd->thk', xb, ue).astype(F32), approximate=False)
        return jnp.einsum('thk,thkd->td', (g * a).astype(ve.dtype), ve)

    y = lax.map(block, x)
    return y.reshape(-1, D_MODEL)[:T].reshape(*lead, D_MODEL)

def layer(h, p_i, conv_prev, attend, g_mix, w_in, b_f, w_dw, b_dw, ln_g, ln_b, w_conv_proj,
          w_att_proj, w_out, g_ffn, w_pq, sub_keys, exp_u, exp_v, g_ple, w_ple, w_ple_gate):
    q, k, v, logf, glu, ga, gc = in_projection(h, g_mix, w_in, b_f)
    att = attend(q, k, v, logf) @ w_att_proj
    glu_ext = jnp.concatenate([conv_prev.astype(glu.dtype), glu], axis=1)
    conv = conv_branch(glu_ext, w_dw, b_dw, ln_g, ln_b, w_conv_proj)
    merged = jax.nn.sigmoid(ga) * att + jax.nn.sigmoid(gc) * conv
    h = h + merged @ w_out
    h = h + peer(rmsnorm(h, g_ffn), w_pq, sub_keys, exp_u, exp_v)
    h = h + (p_i @ w_ple) * jax.nn.sigmoid(rmsnorm(h, g_ple) @ w_ple_gate)
    return h, k, v, logf, glu_ext[:, -(CONV_WIDTH - 1):]

def setup_inputs(seed: int = 0) -> dict:
    key = jax.random.key(seed)
    ks = jax.random.split(key, 32)
    n_pages = PAST_LEN // PAGE_SIZE
    n_pool = (DEC_BATCH * n_pages * 5 + 3) // 4
    nrm = lambda k, shape, s=1.0: jax.random.normal(k, shape, F32) * s
    page_table = jax.random.permutation(ks[0], n_pool)[:DEC_BATCH * n_pages].reshape(DEC_BATCH, n_pages).astype(jnp.int32)
    return {
        'x_prompt': nrm(ks[1], (BATCH, SEQ, D_MODEL)),
        'x_sample': nrm(ks[2], (DEC_BATCH, DEC_SEQ, D_MODEL)),
        'cache_k': nrm(ks[3], (DEPTH, n_pool, PAGE_SIZE, N_HEADS, HEAD_DIM)),
        'cache_v': nrm(ks[4], (DEPTH, n_pool, PAGE_SIZE, N_HEADS, HEAD_DIM)),
        'cache_lf': jax.nn.log_sigmoid(4.0 + nrm(ks[5], (DEPTH, n_pool, PAGE_SIZE, N_HEADS), 0.5)),
        'state_conv': nrm(ks[6], (DEPTH, DEC_BATCH, CONV_WIDTH - 1, CONV_CH)),
        'page_table': page_table,
        'p_prompt': nrm(ks[7], (DEPTH, BATCH, SEQ, PLE_DIM)),
        'p_sample': nrm(ks[8], (DEPTH, DEC_BATCH, DEC_SEQ, PLE_DIM)),
        'g_mix': 1.0 + nrm(ks[9], (DEPTH, D_MODEL), 0.05),
        'w_in': nrm(ks[10], (DEPTH, D_MODEL, IN_COLS), D_MODEL ** -0.5),
        'b_f': 4.0 + nrm(ks[11], (DEPTH, N_HEADS), 0.5),
        'w_dw': nrm(ks[12], (DEPTH, CONV_WIDTH, CONV_CH), CONV_WIDTH ** -0.5),
        'b_dw': nrm(ks[13], (DEPTH, CONV_CH), 0.02),
        'ln_g': 1.0 + nrm(ks[14], (DEPTH, CONV_CH), 0.05),
        'ln_b': nrm(ks[15], (DEPTH, CONV_CH), 0.02),
        'w_conv_proj': nrm(ks[16], (DEPTH, CONV_CH, D_MODEL), CONV_CH ** -0.5),
        'w_att_proj': nrm(ks[17], (DEPTH, ATT_WIDTH, D_MODEL), ATT_WIDTH ** -0.5),
        'w_out': nrm(ks[18], (DEPTH, D_MODEL, D_MODEL), D_MODEL ** -0.5),
        'g_ffn': 1.0 + nrm(ks[19], (DEPTH, D_MODEL), 0.05),
        'w_pq': nrm(ks[20], (DEPTH, D_MODEL, PEER_HEADS * PEER_KEY_DIM), D_MODEL ** -0.5),
        'sub_keys': nrm(ks[21], (DEPTH, 2, N_KEYS, HALF_KEY), HALF_KEY ** -0.5),
        'exp_u': nrm(ks[22], (DEPTH, N_EXPERTS, D_MODEL), D_MODEL ** -0.5),
        'exp_v': nrm(ks[23], (DEPTH, N_EXPERTS, D_MODEL), PEER_HEADS ** -0.5),
        'g_ple': 1.0 + nrm(ks[24], (DEPTH, D_MODEL), 0.05),
        'w_ple': nrm(ks[25], (DEPTH, PLE_DIM, D_MODEL), PLE_DIM ** -0.5),
        'w_ple_gate': nrm(ks[26], (DEPTH, D_MODEL, D_MODEL), D_MODEL ** -0.5),
        'g_final': 1.0 + nrm(ks[27], (D_MODEL,), 0.05),
    }

def reference(x_prompt, x_sample, cache_k, cache_v, cache_lf, state_conv, page_table,
              p_prompt, p_sample, g_mix, w_in, b_f, w_dw, b_dw, ln_g, ln_b, w_conv_proj,
              w_att_proj, w_out, g_ffn, w_pq, sub_keys, exp_u, exp_v, g_ple, w_ple,
              w_ple_gate, g_final):
    hp, hs = x_prompt, x_sample
    kps, vps, lfps, cps = [], [], [], []
    kss, vss, lfss, css = [], [], [], []
    for i in range(DEPTH):
        lw = (g_mix[i], w_in[i], b_f[i], w_dw[i], b_dw[i], ln_g[i], ln_b[i], w_conv_proj[i],
              w_att_proj[i], w_out[i], g_ffn[i], w_pq[i], sub_keys[i], exp_u[i], exp_v[i],
              g_ple[i], w_ple[i], w_ple_gate[i])
        conv0 = jnp.zeros((hp.shape[0], CONV_WIDTH - 1, CONV_CH), hp.dtype)
        hp, kp, vp, lfp, cp = layer(hp, p_prompt[i], conv0, fox_prompt, *lw)
        kps.append(kp); vps.append(vp); lfps.append(lfp); cps.append(cp)
        att_s = functools.partial(fox_sample, cache_k=cache_k[i], cache_v=cache_v[i],
                                  cache_lf=cache_lf[i], page_table=page_table)
        hs, ks_, vs_, lfs_, cs_ = layer(hs, p_sample[i], state_conv[i], att_s, *lw)
        kss.append(ks_); vss.append(vs_); lfss.append(lfs_); css.append(cs_)
    y_prompt = rmsnorm(hp, g_final)
    y_sample = rmsnorm(hs, g_final)
    return (y_prompt, y_sample,
            jnp.stack(kps), jnp.stack(vps), jnp.stack(lfps), jnp.stack(cps),
            jnp.stack(kss), jnp.stack(vss), jnp.stack(lfss), jnp.stack(css))


_drawn_inputs = setup_inputs


def setup_inputs(seed=0):
    import zlib

    import numpy as np

    out = dict(_drawn_inputs(seed))
    spreads = {}
    factors = {'cache_lf': 6.241, 'b_dw': 2.8, 'ln_b': 3.871, 'g_ple': 6.429}
    for name, (base, spread) in spreads.items():
        noise = np.random.default_rng([zlib.crc32(name.encode()), seed]).standard_normal(out[name].shape)
        drawn = base * np.exp(spread * noise) if base else spread * noise
        out[name] = __import__('jax').numpy.asarray(drawn.astype(out[name].dtype))
    for name, factor in factors.items():
        out[name] = (out[name] * factor).astype(out[name].dtype)
    return out
```

```python
import numpy as np
import concourse.bass as bass
from concourse import mybir
from contextlib import ExitStack

F32 = mybir.dt.float32
F32R = mybir.dt.float32r
I32 = mybir.dt.int32
U32 = mybir.dt.uint32
ACT = mybir.ActivationFunctionType
ALU = mybir.AluOpType
AX = mybir.AxisListType
ds = bass.ds

P = 128
D = 1024
KD = D // P
SEQ = 1024
NT = SEQ // P
BD, SD = 8, 4
NS = BD * SD
T = SEQ + NS
NCH = 3
CW = T // NCH
H, DH = 8, 64
AW = H * DH
AC = AW // P
HPC = P // DH
CC = 512
CK = CC // P
CWID = 31
PAD = CWID - 1
PAGE = 128
NPAGES = 32
PH, NK, TOPK = 8, 128, 16
SLOTS = PH * TOPK
PLE = 256
SCALE = DH ** -0.5
RMS_EPS, LN_EPS = 1e-6, 1e-5
NEG = -1e30
LOWEST = -3.0e38
QKV = 3 * AW
COL_CA = QKV + H
COL_CB = COL_CA + CC
COL_GA = COL_CB + CC
COL_GC = COL_GA + D
WS = 4
GRP = 4
NG = BD // GRP
QUAD = 4
NTURN = NPAGES // QUAD
TAPS_K, TAPS_V = 1, (2, 1)

V_MIX, V_FFN, V_PLE, V_FIN, V_BDW, V_LNG, V_LNB = 0, 8, 16, 24, 32, 36, 40
NVEC = 44


class Shared:
    pass


def cols(c):
    return slice(c * CW, (c + 1) * CW)


def flat(ap):
    return ap.rearrange("p a n -> p (a n)")


def hold(eng, sem, value, passed):
    eng.wait_ge(sem, value)
    eng.sem_inc(passed, 1)


class Steps:

    def __init__(self, eng, sem):
        self.eng, self.sem, self.n = eng, sem, 0

    def did(self, ins):
        ins.then_inc(self.sem, 1)
        self.n += 1
        return self.n

    def need(self, n=None):
        self.eng.wait_ge(self.sem, self.n if n is None else n)

    def link(self, ins):
        self.did(ins)
        self.need()

    def restart(self):
        self.eng.sem_clear(self.sem)
        self.n = 0


class Scope:

    def __init__(self, nc, stage):
        self.nc, self.stage, self.ctx, self.sems = nc, stage, ExitStack(), []

    def __enter__(self):
        return self

    def __exit__(self, *a):
        self.ctx.close()
        if self.sems and self.stage != 'all':
            for x in self.sems:
                self.nc.gpsimd.sem_clear(x)
            self.nc.all_engine_barrier()

    def sb(self, name, shape, dt=F32):
        t = self.ctx.enter_context(self.nc.sbuf_tensor(f"{self.stage}_{name}", shape, dt))
        self.end = self.nc.sbuf_base
        return t

    def placed(self, name, shape, dt=F32):
        t = self.sb(name, shape, dt)
        return t, self.end - 4 * int(np.prod(shape[1:]))

    def over(self, name, shape, dt, at):
        return self.nc.alloc_sbuf_tensor_at(f"{self.stage}_{name}", shape, dt, offset=at)

    def ps(self, name, shape=(P, 512)):
        return self.ctx.enter_context(self.nc.psum_tensor(f"{self.stage}_ps_{name}", list(shape), F32))

    def sem(self, name):
        self.sems.append(self.ctx.enter_context(self.nc.semaphore(f"{self.stage}_{name}")))
        return self.sems[-1]

    def block(self):
        return self.ctx.enter_context(self.nc.Block())


def load_tokens(nc, sh, io):
    with Scope(nc, "load") as s:
        xin = s.sb("xin", [P, 2, D])
        vrow, wrow = s.sb("vrow", [NVEC, P]), s.sb("wrow", [CWID * CK, P])
        banks = [[s.ps(f"x{b}{h}") for h in range(2)] for b in range(2)]
        vbank = s.ps("v")
        loaded = [s.sem(f"x_loaded{b}") for b in range(2)]
        vec_loaded, bf_loaded = s.sem("vectors_loaded"), s.sem("bf_loaded")
        turned = [s.sem("low_half_turned"), s.sem("high_half_turned")]
        freed = [s.sem("act_freed"), s.sem("dve_freed")]
        vec_turned, const, passed_a, passed_v = s.sem("vec_turned"), s.sem("const"), s.sem("passed_a"), s.sem("passed_v")
        zeroed = s.sem("zeroed")
        block = s.block()
        xp = io["x_prompt"][0].rearrange("(t p) d -> t p d", p=P)
        xs = io["x_sample"].rearrange("b s d -> (b s) d")

        @block.sync
        def _(sp):
            for b in range(2):
                sp.dma_start(xin[:, b, :], xp[b]).then_inc(loaded[b], 16)
            for row, v, n in ((V_MIX, io["g_mix"], KD), (V_FFN, io["g_ffn"], KD), (V_PLE, io["g_ple"], KD),
                              (V_BDW, io["b_dw"], CK), (V_LNG, io["ln_g"], CK), (V_LNB, io["ln_b"], CK)):
                sp.dma_start(vrow[row:row + n, :], v[0].rearrange("(k p) -> k p", p=P)).then_inc(vec_loaded, 16)
            sp.dma_start(vrow[V_FIN:V_FIN + KD, :], io["g_final"].rearrange("(k p) -> k p", p=P)).then_inc(vec_loaded, 16)
            sp.dma_start(wrow[:, :], io["w_dw"][0].rearrange("w (c p) -> (w c) p", p=P)).then_inc(vec_loaded, 16)
            sp.dma_start(sh.bf[:, :], io["b_f"].rearrange("a h -> h a")).then_inc(bf_loaded, 16)
            with sp.Fori(1, NT // 2) as i:
                for b in range(2):
                    sp.wait_ge(turned[1], 2 * i + b - 1)
                    sp.dma_start(xin[:, b, :], flat(xp[ds(2 * i + b, 1)].rearrange("a p d -> p a d"))).then_inc(loaded[b], 16)
            sp.wait_ge(turned[1], NT - 1)
            sp.dma_start(xin[0:NS, 0, :], xs).then_inc(loaded[0], 16)
            sp.wait_ge(bf_loaded, 16)

        @block.gpsimd
        def _(pool):
            pool.memset(sh.ones[:, :], 1.0).then_inc(const, 1)
            pool.memset(sh.zeros[:, :], 0.0).then_inc(const, 1)
            pool.memset(sh.ident[:, :], 0.0).then_inc(zeroed, 1)
            pool.wait_ge(zeroed, 1)
            pool.affine_select(out=sh.ident[:, :], in_=sh.ident[:, :], compare_op=ALU.not_equal, fill=1.0,
                               base=0, pattern=[[-1, P]], channel_multiplier=1).then_inc(const, 1)

        @block.tensor
        def _(pe):
            pe.wait_ge(const, 3)
            pe.wait_ge(vec_loaded, 16 * 8)
            pe.transpose(vbank[:, 0:NVEC], vrow[:, :], sh.ident[0:NVEC, 0:NVEC])
            n = CWID * CK
            pe.transpose(vbank[:, 64:64 + n], wrow[:, :], sh.ident[0:n, 0:n]).then_inc(vec_turned, 1)
            for f in freed:
                pe.sem_inc(f, 2)
            with pe.Fori(0, NT // 2) as i:
                for b in range(2):
                    pe.wait_ge(loaded[b], 16 * i + 16)
                    for h in range(2):
                        pe.wait_ge(freed[h], 2 * i + b + 1)
                        for k in range(4):
                            last = pe.transpose(banks[b][h][:, k * P:(k + 1) * P],
                                                xin[:, b, (4 * h + k) * P:(4 * h + k + 1) * P], sh.ident[:, :])
                        last.then_inc(turned[h], 1)
            pe.wait_ge(loaded[0], 16 * (NT // 2) + 16)
            for h in range(2):
                pe.wait_ge(freed[h], NT + 1)
                for k in range(4):
                    last = pe.transpose(banks[0][h][:, k * P:k * P + NS],
                                        xin[0:NS, 0, (4 * h + k) * P:(4 * h + k + 1) * P], sh.ident[0:NS, 0:NS])
                last.then_inc(turned[h], 1)

        def copy_out(eng, h, copy, passed):
            with eng.Fori(0, NT // 2) as i:
                for b in range(2):
                    hold(eng, turned[h], 2 * i + b + 1, passed)
                    copy(sh.hT[:, 4 * h:4 * h + 4, ds((2 * i + b) * P, P)],
                         banks[b][h][:, :].rearrange("p (k n) -> p k n", n=P)).then_inc(freed[h], 1)
            eng.wait_ge(turned[h], NT + 1)
            copy(sh.hT[:, 4 * h:4 * h + 4, SEQ:T],
                 banks[0][h][:, :].rearrange("p (k n) -> p k n", n=P)[:, :, 0:NS]).then_inc(freed[h], 1)

        @block.scalar
        def _(act):
            copy_out(act, 0, lambda o, i: act.activation(o, i, ACT.Copy), passed_a)

        @block.vector
        def _(dve):
            dve.wait_ge(vec_turned, 1)
            dve.tensor_copy(sh.vec[:, :], vbank[:, 0:NVEC])
            dve.tensor_copy(sh.wdw[:, :], vbank[:, 64:64 + CWID * CK])
            copy_out(dve, 1, dve.tensor_copy, passed_v)


def rms_norm(nc, sh, name, src, gain, dst):
    with Scope(nc, name) as s:
        r = s.sb("r", [P, NCH, CW])
        banks = [s.ps(f"sum{c}") for c in range(NCH)]
        squared, summed, inverted, rooted, step = (s.sem(x) for x in ("squared", "summed", "inverted", "rooted", "dve_step"))
        block = s.block()

        @block.scalar
        def _(act):
            for c in range(NCH):
                act.activation(dst[:, 0:KD, cols(c)], src[:, :, cols(c)], ACT.Square).then_inc(squared, 1)
            for c in range(NCH):
                act.wait_ge(inverted, c + 1)
                act.activation(r[:, c, :], r[:, c, :], ACT.Sqrt).then_inc(rooted, 1)

        @block.tensor
        def _(pe):
            for c in range(NCH):
                pe.wait_ge(squared, c + 1)
                for k in range(KD):
                    last = pe.matmul(banks[c][:, 0:CW], sh.ones[:, :], dst[:, k, cols(c)], start=k == 0, stop=k == KD - 1)
                last.then_inc(summed, 1)

        @block.vector
        def _(dve):
            st = Steps(dve, step)
            for c in range(NCH):
                dve.wait_ge(summed, c + 1)
                st.link(dve.tensor_scalar(r[:, c, :], banks[c][:, 0:CW], 1.0 / D, RMS_EPS, ALU.mult, ALU.add))
                dve.reciprocal(r[:, c, :], r[:, c, :]).then_inc(inverted, 1)
            for c in range(NCH):
                dve.wait_ge(rooted, c + 1)
                for k in range(KD):
                    dve.scalar_tensor_tensor(out=dst[:, k, cols(c)], in0=src[:, k, cols(c)],
                                             scalar=sh.vec[:, gain + k:gain + k + 1], in1=r[:, c, :],
                                             op0=ALU.mult, op1=ALU.mult)


class Product:

    def __init__(self, nc, s, turns, weights, chunks, rhs, ring=None):
        self.s, self.turns, self.weights, self.chunks, self.rhs = s, turns, weights, chunks, rhs
        self.ring = s.sb("w", [P, WS, KD, P]) if ring is None else ring
        self.banks = [[s.ps(f"b{q}{c}") for c in range(NCH)] for q in range(2)]
        self.loaded = [s.sem(f"w_loaded{j}") for j in range(WS)]
        self.ready = s.sem("products_ready")
        self.free = [s.sem(f"set_free{q}") for q in range(2)]
        self.passed = s.sem("passed_sp")

    def bank(self, j, c):
        return self.banks[j % 2][c][:, 0:CW]

    def ready_at(self, i, j, c):
        return NCH * (WS * i + j) + c + 1

    def frees(self, j, ins):
        ins.then_inc(self.free[j % 2], 1)

    def load_one(self, sp, i, j):
        sp.dma_start(self.ring[:, j, 0:self.chunks[j], :], self.weights(i, j)).then_inc(self.loaded[j], 16)

    def load_next(self, sp, i, j):
        hold(sp, self.ready, self.ready_at(i, j, 0) + NCH - 1 - NCH * WS, self.passed)
        self.load_one(sp, i, j)

    def load(self, sp, start=0):
        for j in range(start, WS):
            self.load_one(sp, 0, j)
        if self.turns > 1:
            with sp.Fori(1, self.turns) as i:
                for j in range(WS):
                    self.load_next(sp, i, j)

    def multiply(self, pe):
        for q in range(2):
            pe.sem_inc(self.free[q], NCH)
        with pe.Fori(0, self.turns) as i:
            for j in range(WS):
                for c in range(NCH):
                    pe.wait_ge(self.free[j % 2], NCH * (2 * i + j // 2) + c + 1)
                    if c == 0:
                        pe.wait_ge(self.loaded[j], 16 * i + 16)
                    for k in range(self.chunks[j]):
                        last = pe.matmul(self.bank(j, c), self.ring[:, j, k, :], self.rhs(j, k, c),
                                         start=k == 0, stop=k == self.chunks[j] - 1)
                    last.then_inc(self.ready, 1)


class SplitProduct(Product):

    def __init__(self, nc, s, turns, weights, chunks, rhs, xs, split=tuple(range(WS)), ring=None, parts_at=None):
        Product.__init__(self, nc, s, turns, weights, chunks, rhs, ring)
        self.split, self.xs = split, [x for x, at in xs]
        if parts_at is None:
            parts = [s.sb(f"w_{p}", [P, 2, KD, P], F32R) for p in ("high", "low")]
        else:
            size = 4 * 2 * KD * P
            parts = [s.over(f"w_{p}", [P, 2, KD, P], F32R, parts_at + n * size) for n, p in enumerate(("high", "low"))]
        self.high, self.low = parts
        self.high_tiles = [s.sb(f"x_high{i}", [P, x.shape[1], T], F32R) for i, (x, at) in enumerate(xs)]
        self.low_tiles = [s.over(f"x_low{i}", [P, x.shape[1], T], F32R, at) for i, (x, at) in enumerate(xs)]
        self.w_high, self.w_split = s.sem("w_high_made"), s.sem("w_split")
        self.x_high, self.x_split = s.sem("x_high_made"), s.sem("x_split")
        self.passed_split = s.sem("passed_split")

    def parts_of(self, x, k, c):
        return self.high_tiles[x][:, k, cols(c)], self.low_tiles[x][:, k, cols(c)]

    def split_weights(self, pool):
        S = len(self.split)

        def one(i, j, first):
            at = self.split.index(j)
            pool.wait_ge(self.loaded[j], 16 * i + 16)
            if not first or at >= 2:
                before = WS * i + self.split[at - 2] if at >= 2 else WS * (i - 1) + self.split[at - 2 + S]
                hold(pool, self.ready, NCH * before + NCH, self.passed_split)
            raw = self.ring[:, j, 0:self.chunks[j], :]
            high, low = self.high[:, at % 2, 0:self.chunks[j], :], self.low[:, at % 2, 0:self.chunks[j], :]
            pool.tensor_copy(high, raw).then_inc(self.w_high, 1)
            hold(pool, self.w_high, S * i + at + 1, self.passed_split)
            pool.tensor_tensor(low, raw, high, ALU.subtract).then_inc(self.w_split, 1)
        for j in self.split:
            one(0, j, True)
        with pool.Fori(1, self.turns) as i:
            for j in self.split:
                one(i, j, False)

    def x_highs(self, act, loaded=None):
        for c in range(NCH):
            if loaded is not None:
                act.wait_ge(loaded[c], 16)
            for x, high in zip(self.xs, self.high_tiles):
                act.activation(high[:, :, cols(c)], x[:, :, cols(c)], ACT.Copy).then_inc(self.x_high, 1)

    def x_lows(self, dve):
        for c in range(NCH):
            for n, (x, high, low) in enumerate(zip(self.xs, self.high_tiles, self.low_tiles)):
                dve.wait_ge(self.x_high, len(self.xs) * c + n + 1)
                dve.tensor_tensor(low[:, :, cols(c)], x[:, :, cols(c)], high[:, :, cols(c)], ALU.subtract).then_inc(self.x_split, 1)

    def restore(self, eng, lo, hi):
        eng.wait_ge(self.ready, NCH * WS * self.turns)
        for x, high, low in zip(self.xs, self.high_tiles, self.low_tiles):
            eng.tensor_tensor(x[:, lo:hi, :], high[:, lo:hi, :], low[:, lo:hi, :], ALU.add)

    def multiply(self, pe):
        S = len(self.split)
        for q in range(2):
            pe.sem_inc(self.free[q], NCH)
        with pe.Fori(0, self.turns) as i:
            for j in range(WS):
                for c in range(NCH):
                    pe.wait_ge(self.free[j % 2], NCH * (2 * i + j // 2) + c + 1)
                    if c == 0:
                        pe.wait_ge(self.loaded[j], 16 * i + 16)
                        if j in self.split:
                            pe.wait_ge(self.w_split, S * i + self.split.index(j) + 1)
                    if j in self.split:
                        pe.wait_ge(self.x_split, len(self.xs) * (c + 1))
                    for k in range(self.chunks[j]):
                        first, end = k == 0, k == self.chunks[j] - 1
                        if j not in self.split:
                            last = pe.matmul(self.bank(j, c), self.ring[:, j, k, :], self.rhs(j, k, c), start=first, stop=end)
                            continue
                        slot = self.split.index(j) % 2
                        w_high, w_low = self.high[:, slot, k, :], self.low[:, slot, k, :]
                        x_high, x_low = self.rhs(j, k, c)
                        pe.matmul(self.bank(j, c), w_high, x_high, start=first, stop=False)
                        pe.matmul(self.bank(j, c), w_high, x_low, start=False, stop=False)
                        last = pe.matmul(self.bank(j, c), w_low, x_high, start=False, stop=end)
                    last.then_inc(self.ready, 1)


def w_view(w):
    return w[0].rearrange("(k p) n -> p k n", p=P)


def project_qkv(nc, sh, io, uT, u_at, qkvT, attT, v_at):
    w = w_view(io["w_in"])
    with Scope(nc, "qkv") as s:
        n = WS * KD * P
        ring = attT[:, :, :].rearrange("p c t -> p (c t)")[:, 0:n].rearrange("p (j k n) -> p j k n", j=WS, k=KD)
        pr = SplitProduct(nc, s, 3, lambda i, j: w[:, :, ds((WS * i + j) * P, P)], [KD] * WS,
                          lambda j, k, c: pr.parts_of(0, k, c), [(uT, u_at)], ring=ring, parts_at=v_at)
        passed_a, passed_v = s.sem("passed_a"), s.sem("passed_v")
        block = s.block()
        block.sync(pr.load)
        block.tensor(pr.multiply)

        def copy_out(eng, mine, copy, passed):
            with eng.Fori(0, 3) as i:
                for j in mine:
                    for c in range(NCH):
                        hold(eng, pr.ready, pr.ready_at(i, j, c), passed)
                        pr.frees(j, copy(flat(qkvT[:, ds(WS * i + j, 1), cols(c)]), pr.bank(j, c)))

        @block.gpsimd
        def _(pool):
            pr.split_weights(pool)
            pr.restore(pool, 6, KD)

        @block.scalar
        def _(act):
            pr.x_highs(act)
            copy_out(act, (0, 2), lambda o, i: act.activation(o, i, ACT.Copy), passed_a)

        @block.vector
        def _(dve):
            pr.x_lows(dve)
            copy_out(dve, (1, 3), dve.tensor_copy, passed_v)
            pr.restore(dve, 0, 6)


def heads_prepare(nc, sh, io, uT, qkvT, qkvS, vtok):
    with Scope(nc, "prep") as s:
        wf = s.sb("wf", [P, KD, H])
        ktok = s.sb("ktok", [P, NT + 1, AW])
        z, a, lf, cum = (s.sb(x, [H, T]) for x in ("z", "a", "lf", "cum"))
        keep = s.sb("keep", [H, NS])
        lftok = s.sb("lftok", [P, NT + 1, H])
        onesrow = s.sb("onesrow", [H, SEQ])
        fb = [s.ps(f"f{c}") for c in range(NCH)]
        kb, vb, lb = [s.ps(f"k{i}") for i in range(2)], [s.ps(f"v{i}") for i in range(2)], s.ps("l")
        names = ("wf_loaded f_ready k_turned v_turned k_copied v_copied lf_turned q_scaled dve_step act_step "
                 "z_ready exp_ready ln_ready keep_made stored rows_stored lf_copied pool_step")
        e = {n: s.sem(n) for n in names.split()}
        block = s.block()
        mx = 32

        @block.sync
        def _(sp):
            sp.dma_start(wf[:, :, :], w_view(io["w_in"])[:, :, QKV:QKV + H]).then_inc(e["wf_loaded"], 16)
            sp.wait_ge(e["q_scaled"], 1)
            for half in range(HPC):
                rows = slice(half * DH, (half + 1) * DH)
                for src, dst in ((0, sh.q_s), (AC, sh.k_s)):
                    sp.dma_start(dst.rearrange("(c e) d t -> e d c t", e=HPC)[half, 0:DH],
                                 qkvT[rows, src:src + AC, 0:SEQ]).then_inc(e["rows_stored"], 16)
            sp.wait_ge(e["ln_ready"], 3)
            sp.dma_start(sh.q_s[:, DH + 1, :], cum[:, 0:SEQ]).then_inc(e["rows_stored"], 16)
            sp.dma_start(sh.k_s[:, DH, :], a[:, 0:SEQ]).then_inc(e["rows_stored"], 16)
            sp.dma_start(sh.q_s[:, DH, :], onesrow[:, :]).then_inc(e["rows_stored"], 16)
            sp.dma_start(sh.k_s[:, DH + 1, :], onesrow[:, :]).then_inc(e["rows_stored"], 16)
            for g in range(NG):
                for q in range(SD):
                    at = SEQ + g * GRP * SD + q
                    sp.dma_start(sh.cum_s[0, g, :, q * GRP:(q + 1) * GRP], cum[:, at:at + SD * (GRP - 1) + 1:SD],
                                 allow_slow_non_contiguous=True).then_inc(e["rows_stored"], 16)
            sp.dma_start(sh.cum_s[1].rearrange("g h x -> h g x"), a[:, SEQ:T].rearrange("h (g x) -> h g x", g=NG)).then_inc(e["rows_stored"], 16)
            sp.wait_ge(e["k_copied"], NT + 1)
            sp.dma_start(io["k_prompt"][0, 0].rearrange("(t p) h d -> p t (h d)", p=P), ktok[:, 0:NT, :]).then_inc(e["stored"], 16)
            sp.dma_start(io["k_sample"][0].rearrange("b s h d -> (b s) (h d)"), ktok[0:NS, NT, :]).then_inc(e["stored"], 16)
            sp.wait_ge(e["v_copied"], NT + 1)
            sp.dma_start(io["v_prompt"][0, 0].rearrange("(t p) h d -> p t (h d)", p=P), vtok[:, 0:NT, :]).then_inc(e["stored"], 16)
            sp.dma_start(io["v_sample"][0].rearrange("b s h d -> (b s) (h d)"), vtok[0:NS, NT, :]).then_inc(e["stored"], 16)
            sp.wait_ge(e["lf_copied"], 1)
            sp.dma_start(io["lf_prompt"][0, 0].rearrange("(t p) h -> p t h", p=P), lftok[:, 0:NT, :]).then_inc(e["stored"], 16)
            sp.dma_start(io["lf_sample"][0].rearrange("b s h -> (b s) h"), lftok[0:NS, NT, :]).then_inc(e["stored"], 16)
            sp.wait_ge(e["rows_stored"], 16 * (9 + NG * SD))
            sp.wait_ge(e["stored"], 16 * 6)

        @block.gpsimd
        def _(pool):
            st = Steps(pool, e["pool_step"])
            st.link(pool.memset(keep[:, :], 1.0))
            pool.memset(keep[:, :].rearrange("h (b s) -> h b s", s=SD)[:, :, 0:1], 0.0).then_inc(e["keep_made"], 1)
            pool.memset(onesrow[:, :], 1.0).then_inc(e["keep_made"], 1)

        @block.tensor
        def _(pe):
            pe.wait_ge(e["wf_loaded"], 16)
            for c in range(NCH):
                for k in range(KD):
                    last = pe.matmul(fb[c][0:H, 0:CW], wf[:, k, :], uT[:, k, cols(c)], start=k == 0, stop=k == KD - 1)
                last.then_inc(e["f_ready"], 1)
            for t in range(NT + 1):
                n = P if t < NT else NS
                for base, bank, turned, copied in ((AC, kb, e["k_turned"], e["k_copied"]), (2 * AC, vb, e["v_turned"], e["v_copied"])):
                    if t >= 2:
                        pe.wait_ge(copied, t - 1)
                    for c in range(AC):
                        last = pe.transpose(bank[t % 2][0:n, c * P:(c + 1) * P], qkvT[:, base + c, t * P:t * P + n], sh.ident[:, :])
                    last.then_inc(turned, 1)
            pe.wait_ge(e["ln_ready"], 1)
            for t in range(NT + 1):
                n = P if t < NT else NS
                last = pe.transpose(lb[0:n, t * H:(t + 1) * H], lf[:, t * P:t * P + n], sh.ident[0:H, 0:H])
            last.then_inc(e["lf_turned"], 1)

        @block.scalar
        def _(act):
            act.activation(qkvT[:, 0:AC, :], qkvT[:, 0:AC, :], ACT.Copy, scale=SCALE).then_inc(e["q_scaled"], 1)
            act.wait_ge(e["z_ready"], 1)
            act.activation(a[:, :], a[:, :], ACT.Exp).then_inc(e["exp_ready"], 1)
            act.wait_ge(e["exp_ready"], 1)
            act.activation(a[:, :], a[:, :], ACT.Ln, bias=1.0).then_inc(e["exp_ready"], 1)
            for t in range(NT + 1):
                n = P if t < NT else NS
                act.wait_ge(e["k_turned"], t + 1)
                act.activation(ktok[0:n, t, :], kb[t % 2][0:n, :], ACT.Copy).then_inc(e["k_copied"], 1)

        @block.vector
        def _(dve):
            st = Steps(dve, e["dve_step"])
            for c in range(NCH):
                dve.wait_ge(e["f_ready"], c + 1)
                st.did(dve.tensor_scalar(z[:, cols(c)], fb[c][0:H, 0:CW], sh.bf[:, 0:1], None, ALU.add))
            st.need()
            st.link(dve.tensor_scalar(a[:, :], z[:, :], -1.0, None, ALU.mult))
            st.link(dve.tensor_tensor(a[:, :], a[:, :], z[:, :], ALU.min))
            dve.tensor_scalar(z[:, :], z[:, :], 0.0, None, ALU.min).then_inc(e["z_ready"], 1)
            dve.wait_ge(e["z_ready"], 1)
            dve.wait_ge(e["exp_ready"], 2)
            dve.tensor_tensor(lf[:, :], z[:, :], a[:, :], ALU.subtract).then_inc(e["ln_ready"], 1)
            dve.wait_ge(e["ln_ready"], 1)
            dve.wait_ge(e["keep_made"], 2)
            st.did(dve.tensor_tensor_scan(cum[:, 0:SEQ], onesrow[:, :], lf[:, 0:SEQ], 0.0, ALU.mult, ALU.add))
            st.link(dve.tensor_tensor_scan(cum[:, SEQ:T], keep[:, :], lf[:, SEQ:T], 0.0, ALU.mult, ALU.add))
            dve.tensor_scalar(a[:, :], cum[:, :], -1.0, None, ALU.mult).then_inc(e["ln_ready"], 2)
            for t in range(NT + 1):
                n = P if t < NT else NS
                dve.wait_ge(e["v_turned"], t + 1)
                dve.tensor_copy(vtok[0:n, t, :], vb[t % 2][0:n, :]).then_inc(e["v_copied"], 1)
            dve.wait_ge(e["q_scaled"], 1)
            dve.tensor_copy(qkvS[:, :, :], qkvT[:, :, SEQ:T])
            dve.wait_ge(e["lf_turned"], 1)
            lbt = lb[:, 0:(NT + 1) * H].rearrange("p (t h) -> p t h", h=H)
            st.link(dve.tensor_copy(lftok[:, 0:NT, :], lbt[:, 0:NT, :]))
            dve.tensor_copy(lftok[0:NS, NT, :], lbt[0:NS, NT, :]).then_inc(e["lf_copied"], 1)


def prompt_attention(nc, sh, io, vtok, attT):
    with Scope(nc, "patt") as s:
        RK = DH + 2
        qh, kh = s.sb("qh", [RK, 2, SEQ]), s.sb("kh", [RK, 2, SEQ])
        mask = s.sb("mask", [P, SEQ])
        sc, pr = s.sb("scores", [P, 2, SEQ]), s.sb("probs", [P, 2, SEQ])
        pT = s.sb("probsT", [P, 2, NT, P])
        att = s.sb("att", [P, NT, AW])
        mx, nm, sm = (s.sb(x, [P, 2]) for x in ("mx", "nm", "sum"))
        rs = s.sb("rsum", [P, 2 * NT])
        sbank = [s.ps(f"s{i}", (P, 1024)) for i in range(2)]
        tbank = [s.ps(f"t{i}") for i in range(2)]
        obank = [s.ps(f"o{i}") for i in range(2)]
        names = ("mask_zeroed mask_made scores_ready masked max_ready exp_ready probs_turned lowT_copied highT_copied "
                 "o_ready o_copied head_done dve_step att_turned att_copied passed_a passed_v passed_sp act_step")
        e = {n: s.sem(n) for n in names.split()}
        loaded = [s.sem(f"qk_loaded{b}") for b in range(2)]
        t_free = [s.sem("t0_free"), s.sem("t1_free")]
        t_ready = [s.sem("t0_ready"), s.sem("t1_ready")]
        block = s.block()
        NST = 2 * NT
        NTURN = H // 2
        blk = [(b, qb) for b in range(2) for qb in range(NT)]
        high = [n for n, (b, qb) in enumerate(blk) if qb >= 4]

        @block.sync
        def _(sp):
            def load(head, b):
                sp.dma_start(qh[:, b, :], head_rows(sh.q_s, head)).then_inc(loaded[b], 16)
                sp.dma_start(kh[:, b, :], head_rows(sh.k_s, head)).then_inc(loaded[b], 16)

            def head_rows(x, head):
                if isinstance(head, int):
                    return x[head]
                return flat(x[ds(head, 1)].rearrange("a d t -> d a t"))
            for b in range(2):
                load(b, b)
            with sp.Fori(1, NTURN) as i:
                for b in range(2):
                    sp.wait_ge(e["scores_ready"], NST * i - NST + NT * (b + 1))
                    load(2 * i + b, b)

        @block.gpsimd
        def _(pool):
            pool.memset(mask[:, :], 0.0).then_inc(e["mask_zeroed"], 1)
            pool.wait_ge(e["mask_zeroed"], 1)
            tri = mask[:, SEQ - P:SEQ]
            pool.affine_select(out=tri, in_=tri, compare_op=ALU.is_ge, fill=NEG, base=0,
                               pattern=[[-1, P]], channel_multiplier=1).then_inc(e["mask_made"], 1)

        @block.tensor
        def _(pe):
            pe.sem_inc(e["masked"], 2)
            pe.sem_inc(e["o_copied"], 2)
            pe.sem_inc(t_free[0], 1)
            pe.sem_inc(t_free[1], 1)
            pe.sem_inc(t_ready[1], 2)

            def scores(i, n):
                b, qb = blk[n]
                if qb == 0:
                    pe.wait_ge(loaded[b], 32 * i + 32)
                pe.wait_ge(e["masked"], NST * i + n + 1)
                width = (qb + 1) * P
                for c0 in range(0, width, 512):
                    c1 = min(width, c0 + 512)
                    last = pe.matmul(sbank[n % 2][:, c0:c1], qh[:, b, qb * P:(qb + 1) * P], kh[:, b, c0:c1],
                                     start=True, stop=True)
                last.then_inc(e["scores_ready"], 1)

            def turn(i, n):
                b, qb = blk[n]
                pe.wait_ge(e["exp_ready"], NST * i + n + 3)
                for half, lo, hi in ((0, 0, min(4, qb + 1)), (1, 4, qb + 1)):
                    if hi <= lo:
                        continue
                    at = n if half == 0 else high.index(n)
                    per = NST if half == 0 else len(high)
                    pe.wait_ge(t_free[half], per * i + at + 1)
                    for kb in range(lo, hi):
                        last = pe.transpose(tbank[half][:, (kb - lo) * P:(kb - lo + 1) * P],
                                            pr[:, n % 2, kb * P:(kb + 1) * P], sh.ident[:, :])
                    last.then_inc(t_ready[half], 1)

            def weigh(i, n):
                b, qb = blk[n]
                pe.wait_ge(t_free[0], NST * i + n + 2)
                if n in high:
                    pe.wait_ge(t_free[1], len(high) * i + high.index(n) + 2)
                pe.wait_ge(e["o_copied"], NST * i + n + 1)
                for kb in range(qb + 1):
                    last = pe.matmul(obank[n % 2][:, 0:DH], pT[:, n % 2, kb, :], vtok[:, kb, ds((2 * i + b) * DH, DH)],
                                     start=kb == 0, stop=kb == qb)
                last.then_inc(e["o_ready"], 1)

            with pe.Fori(0, NTURN) as i:
                for n in range(NST + 2):
                    if n < NST:
                        scores(i, n)
                    if 1 <= n <= NST:
                        turn(i, n - 1)
                    if n >= 2:
                        weigh(i, n - 2)
            for t in range(NT):
                pe.wait_ge(e["o_copied"], NST * NTURN + 2)
                if t >= 2:
                    pe.wait_ge(e["att_copied"], t - 1)
                for c in range(AC):
                    last = pe.transpose(obank[t % 2][:, c * P:(c + 1) * P], att[:, t, c * P:(c + 1) * P], sh.ident[:, :])
                last.then_inc(e["att_turned"], 1)

        @block.scalar
        def _(act):
            def low(i, n):
                b, qb = blk[n]
                w = min(4, qb + 1)
                act.wait_ge(t_ready[0], NST * i + n + 1)
                act.wait_ge(e["o_ready"], NST * i + n + 1)
                act.activation(pT[:, n % 2, 0:w, :], tbank[0][:, 0:w * P].rearrange("p (k n) -> p k n", n=P),
                               ACT.Copy).then_inc(t_free[0], 1)
            act.sem_inc(e["o_ready"], 2)
            act.sem_inc(e["exp_ready"], 2)
            with act.Fori(0, NTURN) as i:
                for n in range(NST + 1):
                    if n < NST:
                        b, qb = blk[n]
                        w = (qb + 1) * P
                        if n < 2:
                            hold(act, t_ready[1], len(high) * i + n + 1, e["passed_a"])
                        elif n - 2 in high:
                            hold(act, t_ready[1], len(high) * i + high.index(n - 2) + 3, e["passed_a"])
                        act.wait_ge(e["max_ready"], NST * i + n + 1)
                        act.activation(pr[:, n % 2, 0:w], sc[:, n % 2, 0:w], ACT.Exp, bias=nm[:, n % 2:n % 2 + 1],
                                       accum_out=sm[:, n % 2:n % 2 + 1]).then_inc(e["exp_ready"], 1)
                    if n >= 1:
                        low(i, n - 1)

        @block.vector
        def _(dve):
            st = Steps(dve, e["dve_step"])
            dve.wait_ge(e["mask_made"], 1)
            with dve.Fori(0, NTURN) as i:
                hold(dve, e["o_copied"], NST * i + 2, e["passed_v"])
                st.restart()
                for n in range(NST + 2):
                    if n < NST:
                        b, qb = blk[n]
                        w = (qb + 1) * P
                        hold(dve, e["scores_ready"], NST * i + n + 1, e["passed_v"])
                        hold(dve, e["exp_ready"], NST * i + n + 1, e["passed_v"])
                        dve.tensor_tensor_reduce(out=sc[:, n % 2, 0:w], in0=sbank[n % 2][:, 0:w],
                                                 in1=mask[:, SEQ - w:SEQ], scale=1.0, scalar=NEG, op0=ALU.add, op1=ALU.max,
                                                 accum_out=mx[:, n % 2:n % 2 + 1]).then_inc(e["masked"], 1)
                        dve.wait_ge(e["masked"], NST * i + n + 3)
                        dve.tensor_scalar(nm[:, n % 2:n % 2 + 1], mx[:, n % 2:n % 2 + 1], -1.0, None,
                                          ALU.mult).then_inc(e["max_ready"], 1)
                    if 1 <= n <= NST:
                        m = n - 1
                        if m in high:
                            w = blk[m][1] + 1 - 4
                            dve.wait_ge(t_ready[1], len(high) * i + high.index(m) + 3)
                            dve.wait_ge(e["o_ready"], NST * i + m + 1)
                            dve.tensor_copy(pT[:, m % 2, 4:4 + w, :], tbank[1][:, 0:w * P].rearrange("p (k n) -> p k n", n=P)
                                            ).then_inc(t_free[1], 1)
                        dve.wait_ge(e["exp_ready"], NST * i + m + 3)
                        st.did(dve.reciprocal(rs[:, m:m + 1], sm[:, m % 2:m % 2 + 1]))
                        rs_at = st.n
                    if n >= 2:
                        m = n - 2
                        b, qb = blk[m]
                        st.need(m + 1)
                        hold(dve, e["o_ready"], NST * i + m + 3, e["passed_v"])
                        dve.tensor_scalar(att[:, qb, ds((2 * i + b) * DH, DH)], obank[m % 2][:, 0:DH],
                                          rs[:, m:m + 1], None, ALU.mult).then_inc(e["o_copied"], 1)
            for t in range(NT):
                dve.wait_ge(e["att_turned"], t + 1)
                dve.tensor_copy(attT[:, 0:AC, t * P:(t + 1) * P], obank[t % 2][:, :].rearrange("p (c n) -> p c n", n=P)
                                ).then_inc(e["att_copied"], 1)


def cache_decay(nc, sh, io):
    with Scope(nc, "decay") as s:
        ptc = s.sb("page_of_row", [P, NG], I32)
        lfp = s.sb("lf_pages", [P, NG, PAGE * H])
        run = s.sb("running", [P, NG, H, PAGE])
        tot = s.sb("totals", [P, NG, H])
        later = s.sb("later", [P, NG, H])
        tri = s.sb("tri", [P, P])
        bank = s.ps("later")
        names = "pt_loaded tri_step tri_made summed later_ready excl_ready stored dve_step"
        e = {n: s.sem(n) for n in names.split()}
        got = sh.lf_gathered
        block = s.block()

        @block.sync
        def _(sp):
            for g in range(NG):
                sp.dma_start(ptc[:, g:g + 1], io["page_table"][GRP * g:GRP * g + GRP].rearrange("b (n a) -> (b n) a", a=1))\
                    .then_inc(e["pt_loaded"], 16)
            for g in range(NG):
                sp.wait_ge(e["excl_ready"], H * (g + 1))
                sp.dma_start(sh.ex_s[g], run[:, g, :, :]).then_inc(e["stored"], 16)
            sp.wait_ge(e["stored"], 16 * NG)

        @block.gpsimd
        def _(pool):
            pool.wait_ge(e["pt_loaded"], 16 * NG)
            for g in range(NG):
                pool.indirect_dma_start(lfp[:, g, :], None, io["cache_lf"][0].rearrange("n k h -> n (k h)"),
                                        bass.IndirectOffsetOnAxis(ptc[:, g:g + 1], 0)).then_inc(got[g], 16)
            st = Steps(pool, e["tri_step"])
            st.link(pool.memset(tri[:, :], 1.0))
            st.link(pool.affine_select(out=tri[:, :], in_=tri[:, :], compare_op=ALU.is_ge, fill=0.0, base=0,
                                       pattern=[[-1, P]], channel_multiplier=1))
            t3 = tri[:, :].rearrange("p (b n) -> p b n", n=NPAGES)
            pool.affine_select(out=t3, in_=t3, compare_op=ALU.is_ge, fill=0.0, base=NPAGES - 1,
                               pattern=[[NPAGES, GRP], [0, NPAGES]], channel_multiplier=-1).then_inc(e["tri_made"], 1)

        @block.vector
        def _(dve):
            st = Steps(dve, e["dve_step"])
            for g in range(NG):
                dve.wait_ge(got[g], 16)
                lf3 = lfp[:, g, :].rearrange("p (k h) -> p h k", h=H)
                for h in range(H):
                    st.did(dve.tensor_tensor_scan(run[:, g, h, :], sh.ones[:, :], lf3[:, h, :], 0.0, ALU.mult, ALU.add))
                st.need()
                dve.tensor_copy(tot[:, g, :], run[:, g, :, PAGE - 1]).then_inc(e["summed"], 1)
            for g in range(NG):
                dve.wait_ge(e["later_ready"], NG)
                st.link(dve.tensor_copy(later[:, g, :], bank[:, g * H:(g + 1) * H]))
                for h in range(H):
                    dve.tensor_scalar(run[:, g, h, :], run[:, g, h, :], -1.0, later[:, g, h:h + 1],
                                      ALU.mult, ALU.add).then_inc(e["excl_ready"], 1)

        @block.tensor
        def _(pe):
            pe.wait_ge(e["tri_made"], 1)
            pe.wait_ge(e["summed"], NG)
            for g in range(NG):
                pe.matmul(bank[:, g * H:(g + 1) * H], tri[:, :], tot[:, g, :], start=True, stop=True)\
                    .then_inc(e["later_ready"], 1)


def conv_taps(sh, done, gp, gs, yT):
    def tap(dve, w, channels=range(CK)):
        first = isinstance(w, int) and w == 0
        for c in channels:
            wc = sh.wdw[:, c:c + 1] if first else sh.wdw[:, ds(w * CK + c, 1)]
            yp = yT[:, c, 0:SEQ]
            ys = yT[:, c, SEQ:T].rearrange("p (b s) -> p b s", s=SD)
            for at, y, x in ((c, yp, gp[:, c, 0:SEQ] if first else gp[:, c, ds(w, SEQ)]),
                             (CK + c, ys, gs[:, c, :, 0:SD] if first else gs[:, c, :, ds(w, SD)])):
                if first:
                    bdw = sh.vec[:, V_BDW + c:V_BDW + c + 1]
                    ins = dve.tensor_scalar(y, x, wc, bdw, ALU.mult, ALU.add)
                else:
                    dve.wait_ge(done[at], w)
                    ins = dve.scalar_tensor_tensor(out=y, in0=x, scalar=wc, in1=y, op0=ALU.mult, op1=ALU.add)
                ins.then_inc(done[at], 1)
    return tap


def sample_attention(nc, sh, io, g, qkvS, attT, taps, start, first, taps_k, taps_v):
    L = NPAGES * PAGE
    W4 = QUAD * PAGE
    NI = NPAGES // QUAD
    t0 = g * GRP * SD
    with Scope(nc, f"satt{g}") as s:
        lg = s.sb("logits", [P, L + SD])
        ring = s.sb("pages", [P, GRP, QUAD, AW])
        kT = s.sb("kT", [P, 2, AC, W4])
        qz = s.sb("qz", [P, AC, GRP, 32])
        cnew = s.sb("cnew", [P, 1])
        table = s.sb("table", [1, GRP * NPAGES], I32)
        vnew = s.sb("vnew", [SD, GRP, AW])
        rowi, rowq = s.sb("rowi", [P, 1], I32), s.sb("rowq", [P, 1])
        colj, m4 = s.sb("colj", [P, SD]), s.sb("m4", [P, SD])
        mx, nm, sm, rs = (s.sb(x, [P, 1]) for x in ("mx", "nm", "sum", "rsum"))
        pc, pT, osb = kT[:, 0, 0:2, :], kT[:, 1, 0:2, :].rearrange("p u (k n) -> p u k n", n=P), kT[:, 0, 2, :]
        pn, pnT = s.sb("pn", [P, SD]), s.sb("pnT", [SD, P])
        tb = [s.ps(f"t{c}") for c in range(AC)]
        sbank, obank, nbank = s.ps("s"), s.ps("o"), s.ps("n")
        names = ("table_loaded bias_loaded small_loaded iota_made row_step q_spread even_turned odd_turned act_copied dve_copied qk_done "
                 "added max_ready exp_ready norm_ready p_turned p_copied pv_done o_ready o_copied out_turned "
                 "pn_ready pn_turned pn_copied dve_step passed_a passed_v passed_s passed_p zeroed sum_inv att_step")
        e = {n: s.sem(n) for n in names.split()}
        HALF = GRP // 2
        page_in = [s.sem(f"pages_loaded{b}") for b in range(HALF)] + sh.pages_loaded[g]

        def load_pages(eng, mine, passed, meanwhile=None):
            regs = [eng.alloc_register(f"page{g}_{mine[0]}_{p}") for p in range(QUAD)]

            def load(cache, i, b):
                eng.load(regs, table[0:1, ds(b * NPAGES + QUAD * i, QUAD)])
                for p in range(QUAD):
                    page = eng.snap(regs[p], min_val=0, max_val=cache.shape[1] - 1)
                    eng.dma_start(ring[:, b, p, :], cache[0, ds(page, 1)].rearrange("a k h d -> k (a h d)"))\
                        .then_inc(page_in[b], 16)
            eng.wait_ge(e["table_loaded"], 16)
            for b in mine:
                load(io["cache_k"], 0, b)
            if meanwhile is not None:
                meanwhile()
            with eng.Fori(1, NI) as i:
                for b in mine:
                    hold(eng, e["odd_turned"], 2 * (GRP * i + b) + 2, passed)
                    load(io["cache_k"], i, b)
            eng.wait_ge(e["odd_turned"], 2 * GRP * NI + 2 * GRP)
            with eng.Fori(0, NI) as i:
                for b in mine:
                    hold(eng, e["pv_done"], GRP * i + b + 1, passed)
                    load(io["cache_v"], i, b)
        block = s.block()

        @block.sync
        def _(sp):
            sp.dma_start(table[:, :], io["page_table"][GRP * g:GRP * g + GRP].rearrange("(a b) n -> a (b n)", a=1))\
                .then_inc(e["table_loaded"], 16)

            def load_small():
                for b in range(GRP):
                    for q in range(SD):
                        row = GRP * q + b
                        sp.dma_start(lg[row::GRP * SD, 0:L].rearrange("h (n k) -> h n k", k=PAGE),
                                     sh.ex_s[g, b * NPAGES:(b + 1) * NPAGES].rearrange("n h k -> h n k")).then_inc(e["bias_loaded"], 16)
                        sp.dma_start(lg[row::GRP * SD, L:L + SD], sh.cum_s[1, g, :, SD * b:SD * b + SD]).then_inc(e["bias_loaded"], 16)
                sp.dma_start(cnew[:, :], sh.cum_s[0, g].rearrange("h (x a) -> (h x) a", a=1)).then_inc(e["small_loaded"], 16)
                sp.dma_start(vnew[:, :, :], io["v_sample"][0, GRP * g:GRP * g + GRP].rearrange("b s h d -> s b (h d)"))\
                    .then_inc(e["small_loaded"], 16)
            load_pages(sp, range(0, HALF), e["passed_s"], load_small)

        @block.gpsimd
        def _(pool):
            pool.memset(qz[:, :, :, :], 0.0).then_inc(e["zeroed"], 1)
            pool.iota(rowi[:, :], [[0, 1]], base=0, channel_multiplier=1).then_inc(e["iota_made"], 1)
            pool.iota(colj[:, :], [[1, SD]], base=0, channel_multiplier=0, allow_small_or_imprecise_dtypes=True)\
                .then_inc(e["iota_made"], 1)
            load_pages(pool, range(HALF, GRP), e["passed_p"])

        @block.tensor
        def _(pe):
            pe.sem_inc(e["odd_turned"], 2 * GRP)
            pe.sem_inc(e["act_copied"], 2)
            pe.sem_inc(e["dve_copied"], 2)
            pe.sem_inc(e["qk_done"], 2)
            pe.sem_inc(e["added"], 1)
            pe.sem_inc(e["pv_done"], GRP)
            pe.sem_inc(e["p_copied"], 2)

            def turn(i, b):
                n = GRP * i + b
                pe.wait_ge(page_in[b], 16 * QUAD * (i + 1))
                for c in range(AC):
                    even = c % 2 == 0
                    pe.wait_ge(e["act_copied"] if even else e["dve_copied"], 2 * n + c // 2 + 1)
                    for p in range(QUAD):
                        last = pe.transpose(tb[c][:, p * P:(p + 1) * P], ring[:, b, p, c * P:(c + 1) * P], sh.ident[:, :])
                    last.then_inc(e["even_turned"] if even else e["odd_turned"], 1)

            def score(i, b):
                n = GRP * i + b
                pe.wait_ge(e["act_copied"], 2 * n + 4)
                pe.wait_ge(e["dve_copied"], 2 * n + 4)
                if b == 0:
                    pe.wait_ge(e["added"], i + 1)
                for c in range(AC):
                    last = pe.matmul(sbank[32 * c:32 * c + 32, :], qz[:, c, b, :], kT[:, b % 2, c, :],
                                     start=b == 0, stop=b == GRP - 1)
                last.then_inc(e["qk_done"], 1)

            pe.wait_ge(e["q_spread"], GRP * HPC)
            with pe.Fori(0, NI) as i:
                turn(i, 0)
                for b in range(1, GRP):
                    turn(i, b)
                    score(i, b - 1)
                score(i, GRP - 1)
            pe.wait_ge(e["added"], NI + 1)
            for b in range(GRP):
                for c in range(AC):
                    last = pe.matmul(sbank[32 * c:32 * c + 32, 0:SD], qz[:, c, b, :],
                                     qkvS[:, AC + c, t0 + SD * b:t0 + SD * b + SD], start=b == 0, stop=b == GRP - 1)
            last.then_inc(e["qk_done"], 1)

            pe.matmul(obank[:, :], sh.zeros[:, 0:P], sh.zeros[:, :], start=True, stop=False)
            with pe.Fori(0, NI // 2) as i:
                for u in range(2):
                    pe.wait_ge(e["norm_ready"], 2 * i + u + 1)
                    pe.wait_ge(e["p_copied"], 2 * i + u + 1)
                    for p in range(QUAD):
                        last = pe.transpose(tb[u][:, p * P:(p + 1) * P], pc[:, u, p * P:(p + 1) * P], sh.ident[:, :])
                    last.then_inc(e["p_turned"], 1)
                    pe.wait_ge(e["p_copied"], 2 * i + u + 3)
                    for b in range(GRP):
                        pe.wait_ge(page_in[b], 16 * QUAD * (NI + 2 * i + u + 1))
                    for p in range(QUAD):
                        for b in range(GRP):
                            last = pe.matmul(obank[32 * b:32 * b + 32, :],
                                             pT[:, u, p, b::GRP],
                                             ring[:, b, p, :], start=False, stop=False, skip_group_check=True)
                            if p == QUAD - 1:
                                last.then_inc(e["pv_done"], 1)
            pe.wait_ge(e["pn_ready"], 1)
            pe.transpose(nbank[0:SD, 0:P], pn[:, :], sh.ident[:, :]).then_inc(e["pn_turned"], 1)
            pe.wait_ge(e["pn_copied"], 1)
            pe.wait_ge(e["small_loaded"], 32)
            for b in range(GRP):
                pe.matmul(obank[32 * b:32 * b + 32, :], pnT[:, b::GRP],
                          vnew[:, b, :], start=False, stop=False, skip_group_check=True)
            pe.matmul(obank[:, :], sh.zeros[:, 0:P], sh.zeros[:, :], start=False, stop=True).then_inc(e["o_ready"], 1)
            pe.wait_ge(e["o_copied"], 1)
            for c in range(AC):
                last = pe.transpose(nbank[:, c * P:(c + 1) * P], osb[:, c * P:(c + 1) * P], sh.ident[:, :])
            last.then_inc(e["out_turned"], 1)

        @block.scalar
        def _(act):
            with act.Fori(0, NI) as i:
                for b in range(GRP):
                    n = GRP * i + b
                    act.wait_ge(e["qk_done"], n + 1)
                    for c in (0, 2):
                        act.wait_ge(e["even_turned"], 2 * n + c // 2 + 1)
                        act.activation(kT[:, b % 2, c, :], tb[c][:, :], ACT.Copy).then_inc(e["act_copied"], 1)
            act.wait_ge(e["max_ready"], 1)
            act.activation(lg[:, :], lg[:, :], ACT.Exp, bias=nm[:, :], accum_out=sm[:, :]).then_inc(e["exp_ready"], 1)
            act.sem_inc(e["p_turned"], 1)
            with act.Fori(0, NI // 2) as i:
                for u in range(2):
                    act.wait_ge(e["p_turned"], 2 * i + u + 2)
                    if u == 0:
                        act.wait_ge(e["pv_done"], GRP * (2 * i) + 1)
                    else:
                        act.wait_ge(e["pv_done"], GRP * (2 * i) + GRP)
                    act.activation(pT[:, u, :, :], tb[u][:, :].rearrange("k (p n) -> k p n", n=P), ACT.Copy)\
                        .then_inc(e["p_copied"], 1)
            act.wait_ge(e["o_ready"], 1)
            act.activation(osb[:, :], obank[:, :], ACT.Copy).then_inc(e["o_copied"], 1)

        @block.vector
        def _(dve):
            st = Steps(dve, e["dve_step"])
            dve.wait_ge(e["zeroed"], 1)
            for half in range(HPC):
                rows = slice(half * DH, half * DH + DH)
                for b in range(GRP):
                    col = half * GRP * SD + b
                    dve.tensor_copy(qz[rows, :, b, col:col + GRP * (SD - 1) + 1:GRP], qkvS[rows, 0:AC, t0 + SD * b:t0 + SD * b + SD])\
                        .then_inc(e["q_spread"], 1)
            dve.wait_ge(e["iota_made"], 2)
            st.link(dve.tensor_scalar(rowi[:, :], rowi[:, :], 2, SD - 1, ALU.logical_shift_right, ALU.bitwise_and))
            st.link(dve.tensor_copy(rowq[:, :], rowi[:, :]))
            st.link(dve.tensor_scalar(m4[:, :], colj[:, :], rowq[:, 0:1], NEG, ALU.is_gt, ALU.mult))
            for w in range(start, first):
                taps(dve, w)
            dve.wait_ge(e["bias_loaded"], 16 * 2 * GRP * SD)
            dve.wait_ge(e["small_loaded"], 32)
            with dve.Fori(0, NI) as i:
                for b in range(GRP):
                    n = GRP * i + b
                    dve.wait_ge(e["qk_done"], n + 1)
                    for c in (1, 3):
                        dve.wait_ge(e["odd_turned"], 2 * n + c // 2 + 1 + 2 * GRP)
                        dve.tensor_copy(kT[:, b % 2, c, :], tb[c][:, :]).then_inc(e["dve_copied"], 1)
                    for part in range(taps_k * b, taps_k * (b + 1)):
                        taps(dve, first + taps_k * i + part // CK, (part % CK,))
                hold(dve, e["qk_done"], GRP * i + GRP + 2, e["passed_v"])
                part = lg[:, ds(i * W4, W4)]
                dve.scalar_tensor_tensor(out=part, in0=sbank[:, :], scalar=cnew[:, 0:1], in1=part,
                                         op0=ALU.add, op1=ALU.add).then_inc(e["added"], 1)
            dve.wait_ge(e["qk_done"], GRP * NI + 3)
            st.link(dve.scalar_tensor_tensor(out=lg[:, L:L + SD], in0=sbank[:, 0:SD], scalar=cnew[:, 0:1],
                                             in1=lg[:, L:L + SD], op0=ALU.add, op1=ALU.add))
            st.link(dve.tensor_tensor(lg[:, L:L + SD], lg[:, L:L + SD], m4[:, :], ALU.add))
            dve.wait_ge(e["added"], NI + 1)
            st.link(dve.reduce_max(mx[:, :], lg[:, :], AX.X))
            dve.tensor_scalar(nm[:, :], mx[:, :], -1.0, None, ALU.mult).then_inc(e["max_ready"], 1)
            dve.wait_ge(e["exp_ready"], 1)
            st.link(dve.reciprocal(rs[:, :], sm[:, :]))
            dve.sem_inc(e["sum_inv"], 1)
            with dve.Fori(0, NI // 2) as i:
                for u in range(2):
                    hold(dve, e["p_turned"], 2 * i + 1, e["passed_v"])
                    dve.tensor_scalar(pc[:, u, :], lg[:, ds((2 * i + u) * W4, W4)], rs[:, 0:1], None, ALU.mult)\
                        .then_inc(e["norm_ready"], 1)
                    for x in range(taps_v):
                        taps(dve, first + taps_k * NI + taps_v * i + x, range(u * CK // 2, (u + 1) * CK // 2))
            dve.tensor_scalar(pn[:, :], lg[:, L:L + SD], rs[:, 0:1], None, ALU.mult).then_inc(e["pn_ready"], 1)
            dve.wait_ge(e["pn_turned"], 1)
            dve.tensor_copy(pnT[:, :], nbank[0:SD, 0:P]).then_inc(e["pn_copied"], 1)
            dve.wait_ge(e["out_turned"], 1)
            for c in range(AC):
                for half in range(HPC):
                    rows = slice(half * DH, half * DH + DH)
                    h = HPC * c + half
                    dve.tensor_copy(attT[rows, c, SEQ + t0:SEQ + t0 + GRP * SD].rearrange("p (b q) -> p b q", b=GRP),
                                    nbank[rows, c * P:(c + 1) * P].rearrange("p (b h q) -> p h b q", b=GRP, h=H)[:, h])


def glu_inputs(nc, sh, io, uT, u_at, gp, gs, yT):
    w = w_view(io["w_in"])
    with Scope(nc, "glu") as s:
        start = (COL_CB, COL_CA)
        ring = yT[:, :, :].rearrange("p c t -> p (c t)")[:, 0:WS * KD * P].rearrange("p (j k n) -> p j k n", j=WS, k=KD)
        pr = SplitProduct(nc, s, CK // 2, lambda i, j: w[:, :, ds(start[j % 2] + (2 * i + j // 2) * P, P)], [KD] * WS,
                          lambda j, k, c: pr.parts_of(0, k, c), [(uT, u_at)], ring=ring)
        sg = s.sb("sg", [P, 2, T])
        past = s.sb("past", [BD * PAD // 2, 2, CC])
        tok = s.sb("tok", [NS, CC])
        tokp = s.sb("tokp", [PAD, CC])
        names = "sig_ready sig_used runs_made zeroed past_loaded past_turned past_copied tok_turned tok_copied stored passed_a passed_v"
        e = {n: s.sem(n) for n in names.split()}
        pb = [s.ps("p0"), s.ps("p1")]
        block = s.block()
        HB = BD // 2

        @block.sync
        def _(sp):
            sp.dma_start(past[:, :, :], io["state_conv"][0].rearrange("(a b) w c -> (b w) a c", a=2)).then_inc(e["past_loaded"], 16)
            pr.load(sp)
            sp.dma_start(io["conv_sample"][0, :, 0:PAD - SD], io["state_conv"][0, :, SD:PAD]).then_inc(e["stored"], 16)
            sp.wait_ge(e["tok_copied"], 2)
            sp.dma_start(io["conv_sample"][0, :, PAD - SD:PAD], tok[:, :]).then_inc(e["stored"], 16)
            sp.dma_start(io["conv_prompt"][0, 0], tokp[:, :]).then_inc(e["stored"], 16)
            sp.wait_ge(e["stored"], 48)

        @block.gpsimd
        def _(pool):
            pool.memset(gp[:, :, 0:PAD], 0.0).then_inc(e["zeroed"], 1)
            pr.split_weights(pool)
            pr.restore(pool, 6, KD)

        @block.tensor
        def _(pe):
            pe.wait_ge(e["past_loaded"], 16)
            for a in range(2):
                for c in range(CK):
                    n = BD * PAD // 2
                    last = pe.transpose(pb[a][:, c * P:c * P + n], past[:, a, c * P:(c + 1) * P], sh.ident[0:n, 0:n])
                last.then_inc(e["past_turned"], 1)
            pr.multiply(pe)
            pe.wait_ge(e["runs_made"], 1)
            pe.wait_ge(e["past_copied"], 2)
            for c in range(CK):
                pe.transpose(pb[0][0:PAD, c * P:(c + 1) * P], gp[:, c, SEQ:SEQ + PAD], sh.ident[:, :])
            for c in range(CK):
                last = pe.transpose(pb[1][0:NS, c * P:(c + 1) * P], sg[:, 0, c * NS:(c + 1) * NS], sh.ident[:, :])
            last.then_inc(e["tok_turned"], 1)

        @block.scalar
        def _(act):
            pr.x_highs(act)
            act.sem_inc(e["sig_used"], 2)
            with act.Fori(0, CK // 2) as i:
                for j in (0, 2):
                    act.wait_ge(e["sig_used"], 2 * i + j // 2 + 1)
                    for c in range(NCH):
                        act.wait_ge(pr.ready, pr.ready_at(i, j, c))
                        a = act.activation(sg[:, j // 2, cols(c)], pr.bank(j, c), ACT.Sigmoid)
                        pr.frees(j, a)

        @block.vector
        def _(dve):
            pr.x_lows(dve)
            dve.wait_ge(e["past_turned"], 2)
            for a in range(2):
                for c in range(CK):
                    last = dve.tensor_copy(gs[:, c, HB * a:HB * a + HB, 0:PAD],
                                           pb[a][:, c * P:c * P + BD * PAD // 2].rearrange("p (b w) -> p b w", w=PAD))
                last.then_inc(e["past_copied"], 1)
            with dve.Fori(0, CK // 2) as i:
                for j in (1, 3):
                    for c in range(NCH):
                        hold(dve, pr.free[0], NCH * (2 * i + j // 2) + NCH + c + 1, e["passed_v"])
                        hold(dve, pr.ready, pr.ready_at(i, j, c), e["passed_v"])
                        n = min(CW, SEQ - c * CW)
                        pr_bank = pr.bank(j, c)
                        x = dve.tensor_tensor(flat(gp[:, ds(2 * i + j // 2, 1), PAD + c * CW:PAD + c * CW + n]),
                                              pr_bank[:, 0:n], sg[:, j // 2, c * CW:c * CW + n], ALU.mult)
                        if n == CW:
                            pr.frees(j, x)
                            continue
                        pr.frees(j, dve.tensor_tensor(
                            gs[:, ds(2 * i + j // 2, 1), :, PAD:PAD + SD].rearrange("p a b s -> p (a b) s"),
                            pr_bank[:, n:CW].rearrange("p (b s) -> p b s", s=SD),
                            sg[:, j // 2, SEQ:T].rearrange("p (b s) -> p b s", s=SD), ALU.mult))
                    dve.wait_ge(pr.free[1], NCH * (2 * i + j // 2) + 2 * NCH)
                    dve.sem_inc(e["sig_used"], 1)
            dve.wait_ge(pr.free[1], NCH * (CK + 1))
            for c in range(CK):
                last = dve.tensor_copy(sg[:, 0, c * NS:(c + 1) * NS].rearrange("p (b s) -> p b s", s=SD), gs[:, c, :, PAD:PAD + SD])
            last.then_inc(e["runs_made"], 1)
            pr.restore(dve, 0, 6)
            dve.wait_ge(e["tok_turned"], 1)
            dve.tensor_copy(tokp[:, :], pb[0][0:PAD, :]).then_inc(e["tok_copied"], 1)
            dve.tensor_copy(tok[:, :], pb[1][0:NS, :]).then_inc(e["tok_copied"], 1)


def conv_norm(nc, sh, yT):
    with Scope(nc, "ln") as s:
        sq = s.sb("sq", [P, CK, T])
        r = s.sb("r", [P, NCH, CW])
        mb = [s.ps(f"m{c}") for c in range(NCH)]
        vb = [s.ps(f"v{c}") for c in range(NCH)]
        names = "mean_ready centred squared var_ready inverted rooted scaled dve_step act_step made"
        e = {n: s.sem(n) for n in names.split()}
        block = s.block()

        @block.tensor
        def _(pe):
            for c in range(NCH):
                for k in range(CK):
                    last = pe.matmul(mb[c][:, 0:CW], sh.ones[:, :], yT[:, k, cols(c)], start=k == 0, stop=k == CK - 1)
                last.then_inc(e["mean_ready"], 1)
            for c in range(NCH):
                pe.wait_ge(e["squared"], c + 1)
                for k in range(CK):
                    last = pe.matmul(vb[c][:, 0:CW], sh.ones[:, :], sq[:, k, cols(c)], start=k == 0, stop=k == CK - 1)
                last.then_inc(e["var_ready"], 1)

        @block.vector
        def _(dve):
            st = Steps(dve, e["dve_step"])
            for c in range(NCH):
                dve.wait_ge(e["mean_ready"], c + 1)
                for k in range(CK):
                    last = dve.scalar_tensor_tensor(out=yT[:, k, cols(c)], in0=mb[c][:, 0:CW], scalar=-1.0 / CC,
                                                    in1=yT[:, k, cols(c)], op0=ALU.mult, op1=ALU.add)
                last.then_inc(e["centred"], 1)
            for c in range(NCH):
                dve.wait_ge(e["var_ready"], c + 1)
                st.link(dve.tensor_scalar(r[:, c, :], vb[c][:, 0:CW], 1.0 / CC, LN_EPS, ALU.mult, ALU.add))
                dve.reciprocal(r[:, c, :], r[:, c, :]).then_inc(e["inverted"], 1)
            dve.wait_ge(e["centred"], NCH)
            for c in range(NCH):
                dve.wait_ge(e["rooted"], c + 1)
                for k in range(CK):
                    dve.scalar_tensor_tensor(out=yT[:, k, cols(c)], in0=yT[:, k, cols(c)],
                                             scalar=sh.vec[:, V_LNG + k:V_LNG + k + 1], in1=r[:, c, :],
                                             op0=ALU.mult, op1=ALU.mult).then_inc(e["scaled"], 1)
            for k in range(CK):
                dve.wait_ge(e["made"], k + 1)
                dve.scalar_tensor_tensor(out=yT[:, k, :], in0=yT[:, k, :], scalar=sh.vec[:, V_LNB + k:V_LNB + k + 1],
                                         in1=sq[:, k, :], op0=ALU.add, op1=ALU.mult)

        @block.scalar
        def _(act):
            for c in range(NCH):
                act.wait_ge(e["centred"], c + 1)
                act.activation(sq[:, :, cols(c)], yT[:, :, cols(c)], ACT.Square).then_inc(e["squared"], 1)
            for c in range(NCH):
                act.wait_ge(e["inverted"], c + 1)
                act.activation(r[:, c, :], r[:, c, :], ACT.Sqrt).then_inc(e["rooted"], 1)
            act.wait_ge(e["scaled"], NCH * CK)
            act.wait_ge(e["var_ready"], NCH)
            for k in range(CK):
                act.activation(sq[:, k, :], yT[:, k, :], ACT.Sigmoid, bias=sh.vec[:, V_LNB + k:V_LNB + k + 1]).then_inc(e["made"], 1)


def merge(nc, sh, io, uT, u_at, attT, yT):
    wi, wa, wc = w_view(io["w_in"]), w_view(io["w_att_proj"]), w_view(io["w_conv_proj"])
    with Scope(nc, "merge") as s:
        def weights(i, j):
            return (wi[:, :, ds(COL_GA + i * P, P)], wa[:, :, ds(i * P, P)],
                    wi[:, :, ds(COL_GC + i * P, P)], wc[:, :, ds(i * P, P)])[j]

        def rhs(j, k, c):
            return pr.parts_of(0, k, c) if j % 2 == 0 else (attT, yT)[j // 2][:, k, cols(c)]
        pr = SplitProduct(nc, s, KD, weights, [KD, AC, KD, CK], rhs, [(uT, u_at)], split=(0, 2))
        sg = s.sb("sg", [P, 2, T])
        tmp, row = s.sb("tmp", [P, T]), s.sb("row", [P, T])
        passed_v, used = s.sem("passed_v"), s.sem("sig_used")
        mixed, stored, passed_s = s.sem("mixed"), s.sem("stored"), s.sem("passed_s")
        block = s.block()
        block.tensor(pr.multiply)
        block.gpsimd(pr.split_weights)

        @block.sync
        def _(sp):
            def store(i):
                hold(sp, mixed, NCH * i + NCH, passed_s)
                sp.dma_start(sh.m_s[:, ds(i, 1), :].rearrange("p a n -> p (a n)"), row[:, :]).then_inc(stored, 16)
            for j in range(WS):
                pr.load_one(sp, 0, j)
            with sp.Fori(1, KD) as i:
                for j in range(WS):
                    pr.load_next(sp, i, j)
                store(i - 1)
            store(KD - 1)
            sp.wait_ge(stored, 16 * KD + 16)

        @block.scalar
        def _(act):
            pr.x_highs(act)
            act.sem_inc(used, 2)
            with act.Fori(0, KD) as i:
                for j in (0, 2):
                    for c in range(NCH):
                        if c == 0:
                            act.wait_ge(used, 2 * i + j // 2 + 1)
                        act.wait_ge(pr.ready, pr.ready_at(i, j, c))
                        pr.frees(j, act.activation(sg[:, j // 2, cols(c)], pr.bank(j, c), ACT.Sigmoid))

        @block.vector
        def _(dve):
            pr.x_lows(dve)
            dve.sem_inc(stored, 16)
            with dve.Fori(0, KD) as i:
                m = [row[:, cols(c)] for c in range(NCH)]
                hold(dve, stored, 16 * i + 16, passed_v)
                for j in (1, 3):
                    for c in range(NCH):
                        hold(dve, pr.free[0], NCH * (2 * i + j // 2) + NCH + c + 1, passed_v)
                        hold(dve, pr.ready, pr.ready_at(i, j, c), passed_v)
                        dst = m[c] if j == 1 else tmp[:, cols(c)]
                        pr.frees(j, dve.tensor_tensor(dst, pr.bank(j, c), sg[:, j // 2, cols(c)], ALU.mult))
                    hold(dve, pr.free[1], NCH * (2 * i + j // 2) + 2 * NCH, passed_v)
                    dve.sem_inc(used, 1)
                for c in range(NCH):
                    dve.tensor_tensor(m[c], m[c], tmp[:, cols(c)], ALU.add).then_inc(mixed, 1)
                hold(dve, mixed, NCH * i + NCH, passed_v)


def residual_product(nc, sh, name, weight, xT, x_at):
    w = w_view(weight)
    with Scope(nc, name) as s:
        pr = SplitProduct(nc, s, KD // WS, lambda i, j: w[:, :, ds((WS * i + j) * P, P)], [KD] * WS,
                          lambda j, k, c: pr.parts_of(0, k, c), [(xT, x_at)])
        passed_v, x_loaded = s.sem("passed_v"), [s.sem(f"x_loaded{c}") for c in range(NCH)]
        block = s.block()
        block.tensor(pr.multiply)
        block.gpsimd(pr.split_weights)

        @block.sync
        def _(sp):
            for c in range(NCH):
                sp.dma_start(xT[:, :, cols(c)], sh.m_s[:, :, cols(c)]).then_inc(x_loaded[c], 16)
                if c == 0:
                    pr.load_one(sp, 0, 0)
            pr.load(sp, 1)

        @block.scalar
        def _(act):
            pr.x_highs(act, x_loaded)

        @block.vector
        def _(dve):
            pr.x_lows(dve)
            with dve.Fori(0, KD // WS) as i:
                for j in range(WS):
                    for c in range(NCH):
                        hold(dve, pr.ready, pr.ready_at(i, j, c), passed_v)
                        h = flat(sh.hT[:, ds(WS * i + j, 1), cols(c)])
                        pr.frees(j, dve.tensor_tensor(h, pr.bank(j, c), h, ALU.add))


REP = P // NS


def key_weights(nc, sh, io, uT, wk):
    w = w_view(io["w_pq"])
    NQ = 2 * PH
    HK = KD // 2
    with Scope(nc, "keys") as s:
        ring = s.sb("w", [P, WS, KD, P])
        wT = s.sb("wT", [P, 2, KD, P])
        sk, skT = s.sb("sk", [P, 2, P]), s.sb("skT", [P, 2, P])
        tb = [[s.ps(f"t{b}{f}") for f in range(2)] for b in range(2)]
        ob = [[s.ps(f"o{b}{f}") for f in range(2)] for b in range(2)]
        loaded = [s.sem(f"w_loaded{j}") for j in range(WS)]
        names = "sk_loaded sk_turned sk_copied turned multiplied passed_s"
        e = {n: s.sem(n) for n in names.split()}
        wT_made = [s.sem("wT_made_act"), s.sem("wT_made_dve")]
        wk_made = [s.sem("wk_made_act"), s.sem("wk_made_dve")]
        passed = [s.sem("passed_a"), s.sem("passed_v")]
        stored = sh.tokens_stored
        block = s.block()

        @block.sync
        def _(sp):
            def one(i, j):
                sp.dma_start(ring[:, j, :, :], w[:, :, ds((WS * i + j) * P, P)]).then_inc(loaded[j], 16)
            sp.dma_start(sk[:, :, :], io["sub_keys"][0].rearrange("a n d -> n a d")).then_inc(e["sk_loaded"], 16)
            for j in range(WS):
                one(0, j)
            with sp.Fori(1, NQ // WS) as i:
                for j in range(WS):
                    hold(sp, e["turned"], WS * i + j + 1 - WS, e["passed_s"])
                    one(i, j)

        @block.gpsimd
        def _(pool):
            for t in range(NT):
                pool.dma_start(sh.u_s[t], uT[:, :, t * P:(t + 1) * P]).then_inc(stored, 16)
            for r in range(REP):
                pool.dma_start(sh.u_s[NT, :, :, r * NS:(r + 1) * NS], uT[:, :, SEQ:T]).then_inc(stored, 16)
            pool.wait_ge(stored, 16 * (NT + REP))

        @block.tensor
        def _(pe):
            for x in wT_made + wk_made:
                pe.sem_inc(x, 2)
            pe.sem_inc(e["multiplied"], 2)
            pe.wait_ge(e["sk_loaded"], 16)
            for a in range(2):
                last = pe.transpose(ob[0][0][:, a * P:(a + 1) * P], sk[:, a, :], sh.ident[:, :])
            last.then_inc(e["sk_turned"], 1)
            pe.wait_ge(e["sk_copied"], 1)

            def turn(i, j):
                n = WS * i + j
                pe.wait_ge(loaded[j], 16 * i + 16)
                for f in range(2):
                    pe.wait_ge(wT_made[f], n + 1)
                    for k in range(HK):
                        last = pe.transpose(tb[j % 2][f][:, k * P:(k + 1) * P], ring[:, j, HK * f + k, :], sh.ident[:, :])
                last.then_inc(e["turned"], 1)

            def multiply(i, j):
                n = WS * i + j
                for f in range(2):
                    pe.wait_ge(wT_made[f], n + 3)
                    pe.wait_ge(wk_made[f], n + 1)
                    for k in range(HK):
                        last = pe.matmul(ob[j % 2][f][:, k * P:(k + 1) * P], wT[:, j % 2, HK * f + k, :], skT[:, j % 2, :],
                                         start=True, stop=True)
                last.then_inc(e["multiplied"], 1)
            with pe.Fori(0, NQ // WS) as i:
                turn(i, 0)
                for j in range(WS):
                    if j + 1 < WS:
                        turn(i, j + 1)
                    multiply(i, j)

        def copies(eng, f, copy):
            def take_turned(i, j):
                n = WS * i + j
                eng.wait_ge(e["multiplied"], n + 1)
                hold(eng, e["turned"], n + 1, passed[f])
                copy(wT[:, j % 2, HK * f:HK * f + HK, :], tb[j % 2][f][:, :].rearrange("p (k n) -> p k n", n=P)).then_inc(wT_made[f], 1)

            def take_product(i, j):
                n = WS * i + j
                hold(eng, e["multiplied"], n + 3, passed[f])
                copy(wk[:, HK * f:HK * f + HK, ds(n, 1), :].rearrange("p k a n -> p (k a) n"),
                     ob[j % 2][f][:, :].rearrange("p (k n) -> p k n", n=P)).then_inc(wk_made[f], 1)
            with eng.Fori(0, NQ // WS) as i:
                take_turned(i, 0)
                for j in range(WS):
                    if j + 1 < WS:
                        take_turned(i, j + 1)
                    take_product(i, j)

        @block.scalar
        def _(act):
            copies(act, 0, lambda o, i: act.activation(o, i, ACT.Copy))

        @block.vector
        def _(dve):
            dve.wait_ge(e["sk_turned"], 1)
            dve.tensor_copy(skT[:, :, :], ob[0][0][:, 0:2 * P].rearrange("p (a n) -> p a n", n=P)).then_inc(e["sk_copied"], 1)
            copies(dve, 1, dve.tensor_copy)


def experts(nc, sh, io, wk):
    NU, NV, ND = 8, 8, 4
    U0, V0, G0 = NU, NV + TOPK, 1
    NC_ = 70
    blocks = [(0, 2, 16), (2, 8, 5), (8, 16, 1)]
    with Scope(nc, "exp") as s:
        ust = s.sb("ust", [P, KD, P])
        xbn, xb = s.sb("x_next", [P, D]), s.sb("x", [P, D])
        sc = s.sb("scores", [P, 2 * PH, P])
        s1, s2 = s.sb("s1", [P, 2, P]), s.sb("s2", [P, 2, P])
        sv, si, sif = s.sb("sv", [P, 2, TOPK]), s.sb("si", [P, 2, TOPK], U32), s.sb("sif", [P, 2, TOPK])
        sbase = s.sb("sbase", [P, TOPK])
        cand, cand2, cidx = s.sb("cand", [P, NC_]), s.sb("cand2", [P, NC_]), s.sb("cidx", [P, NC_])
        iota = s.sb("iota", [P, NC_])
        tv, ti, tif, ntv = s.sb("tv", [P, TOPK]), s.sb("ti", [P, TOPK], U32), s.sb("tif", [P, TOPK]), s.sb("ntv", [P, 1])
        picked, ef = s.sb("picked", [P, TOPK, NC_]), s.sb("ef", [P, TOPK])
        idx_next, idx_cur = s.sb("idx_next", [P, SLOTS], I32), s.sb("idx_cur", [P, SLOTS], I32)
        idx_now = s.sb("idx_now", [P, 2, TOPK], I32)
        ge, gsum, grec, gate = s.sb("ge", [P, SLOTS]), s.sb("gsum", [P, PH]), s.sb("grec", [P, PH]), s.sb("gate", [P, SLOTS])
        dots, act_dots, wt = s.sb("dots", [P, TOPK]), s.sb("act_dots", [P, TOPK]), s.sb("wt", [P, TOPK])
        U, V = s.sb("U", [P, NU, D]), s.sb("V", [P, NV, D])
        diag = s.sb("diag", [P, ND, P])
        fold = s.sb("fold", [P, P])
        ysb = s.sb("y", [P, D])
        scb = s.ps("sc")
        xt = [s.ps(f"x{i}") for i in range(2)]
        yb = [s.ps(f"y{i}") for i in range(2)]
        names = ("stage_loaded sc_ready sc_copied xb_turned xb_copied tv_ready gate_done "
                 "idx_ready advanced staged u_free v_free gelu_done w_ready diag_ready y_ready y_copied y_turned y_added "
                 "chain adv iota_made fold_zeroed fold_made passed_p passed_a passed_v passed_t passed_s")
        e = {n: s.sem(n) for n in names.split()}
        u_in, v_in = sh.u_loaded, sh.v_loaded
        block = s.block()
        HS = SLOTS // REP // TOPK

        @block.sync
        def _(sp):
            sp.dma_start(ust[:, :, :], sh.u_s[0]).then_inc(e["stage_loaded"], 16)
            with sp.Fori(1, NT + 1) as t:
                hold(sp, e["sc_ready"], PH * t, e["passed_s"])
                hold(sp, e["xb_turned"], 2 * t, e["passed_s"])
                sp.dma_start(ust[:, :, :], sh.u_s[ds(t, 1)].rearrange("a p m n -> p (a m) n")).then_inc(e["stage_loaded"], 16)

        @block.gpsimd
        def _(pool):
            pool.iota(iota[:, :], [[1, NC_]], base=0, channel_multiplier=0, allow_small_or_imprecise_dtypes=True)\
                .then_inc(e["iota_made"], 1)
            pool.memset(fold[:, :], 0.0).then_inc(e["fold_zeroed"], 1)

            def head(n, col, hh):
                hold(pool, e["v_free"], V0 + TOPK * (n - 1), e["passed_p"])
                pool.tensor_copy(idx_now[:, hh, :], idx_cur[:, col]).then_inc(e["staged"], 1)
                hold(pool, e["staged"], n + 1, e["passed_p"])
                for table, buf, ring, free, first, size in ((io["exp_u"], U, u_in, e["u_free"], U0, NU),
                                                            (io["exp_v"], V, v_in, e["v_free"], V0, NV)):
                    for k in range(TOPK):
                        if k % 2 == 0:
                            hold(pool, free, TOPK * n + k + 1 + first - size + 1, e["passed_p"])
                        pool.indirect_dma_start(buf[:, k % size, :], None, table[0],
                                                bass.IndirectOffsetOnAxis(idx_now[:, hh, k:k + 1], 0))\
                            .then_inc(ring[k % size], 16)
            with pool.Fori(0, NT) as t:
                hold(pool, e["idx_ready"], t + 1, e["passed_p"])
                with pool.Fori(0, PH // 2) as h2:
                    for hh in range(2):
                        head(PH * t + 2 * h2 + hh, ds((2 * h2 + hh) * TOPK, TOPK), hh)
            pool.wait_ge(e["idx_ready"], NT + 1)
            for hh in range(HS):
                head(PH * NT + hh, slice(hh * TOPK, (hh + 1) * TOPK), hh % 2)

        @block.tensor
        def _(pe):
            pe.sem_inc(e["v_free"], V0)
            pe.sem_inc(e["y_copied"], 1)
            pe.sem_inc(e["y_turned"], 2)
            pe.sem_inc(e["y_added"], 2)
            pe.sem_inc(e["sc_copied"], 1)

            def turn_tokens(t):
                pe.wait_ge(e["stage_loaded"], 16 * t + 16)
                pe.wait_ge(e["y_added"], 2 if isinstance(t, int) and t == 0 else 2 * t)
                for f in range(2):
                    for k in range(4):
                        last = pe.transpose(xt[f][:, k * P:(k + 1) * P], ust[:, 4 * f + k, :], sh.ident[:, :])
                    last.then_inc(e["xb_turned"], 1)

            def score(t, q, h):
                pe.wait_ge(e["stage_loaded"], 16 * t + 16)
                pe.wait_ge(e["sc_copied"], q + 1)
                for k in range(KD):
                    last = pe.matmul(scb[:, 0:2 * P].rearrange("p (a n) -> p a n", n=P), ust[:, k, :], wk[:, k, ds(2 * h, 2), :],
                                     start=k == 0, stop=k == KD - 1)
                last.then_inc(e["sc_ready"], 1)

            def weigh(n):
                for k in range(TOPK):
                    g = TOPK * n + k
                    pe.wait_ge(e["diag_ready"], G0 + g + 1)
                    pe.wait_ge(v_in[k % NV], 16 * ((TOPK // NV) * n + k // NV + 1))
                    for f in range(2):
                        last = pe.matmul(yb[f][:, :], diag[:, k % ND, :], V[:, k % NV, f * 512:(f + 1) * 512],
                                         start=False, stop=False, skip_group_check=True)
                    last.then_inc(e["v_free"], 1)

            def begin(t):
                pe.wait_ge(e["y_copied"], t + 1)
                for f in range(2):
                    pe.matmul(yb[f][:, :], sh.zeros[:, 0:P], sh.zeros[:, :], start=True, stop=False, skip_group_check=True)

            def end(t):
                for f in range(2):
                    last = pe.matmul(yb[f][:, :], sh.zeros[:, 0:P], sh.zeros[:, :], start=False, stop=True, skip_group_check=True)
                last.then_inc(e["y_ready"], 1)
                pe.wait_ge(e["y_copied"], t + 2)
                for f in range(2):
                    for k in range(4):
                        last = pe.transpose(xt[f][:, k * P:(k + 1) * P], ysb[:, (4 * f + k) * P:(4 * f + k + 1) * P], sh.ident[:, :])
                    last.then_inc(e["y_turned"], 1)

            turn_tokens(0)
            with pe.Fori(0, PH) as h:
                score(0, h, h)
            score(1, PH, 0)
            def tile(t, last):
                begin(t)
                score(t + 1, PH * t + PH + 1, 1)
                weigh(PH * t)
                pe.wait_ge(e["xb_copied"], 2 * t + 2)
                turn_tokens(t + 1)
                with pe.Fori(1, PH - 1) as h:
                    score(t + 1, PH * t + PH + h + 1, h + 1)
                    weigh(PH * t + h)
                if not last:
                    score(t + 2, PH * t + 2 * PH, 0)
                weigh(PH * t + PH - 1)
                pe.wait_ge(e["xb_copied"], 2 * t + 4)
                end(t)
            with pe.Fori(0, NT - 1) as t:
                tile(t, False)
            tile(NT - 1, True)
            begin(NT)
            for hh in range(HS):
                weigh(PH * NT + hh)
            end(NT)

        @block.scalar
        def _(act):
            act.sem_inc(e["gate_done"], 1)
            act.sem_inc(e["diag_ready"], G0)
            act.sem_inc(e["gelu_done"], 1)

            def take_tokens(t):
                for f in range(2):
                    act.wait_ge(e["xb_turned"], 2 * t + f + 1)
                    act.activation(xbn[:, f * 512:(f + 1) * 512], xt[f][:, :], ACT.Copy).then_inc(e["xb_copied"], 1)

            def take_scores(q, h):
                hold(act, e["sc_ready"], q + 1, e["passed_a"])
                act.activation(sc[:, ds(2 * h, 2), :], scb[:, 0:2 * P].rearrange("p (m n) -> p m n", n=P), ACT.Copy)\
                    .then_inc(e["sc_copied"], 1)

            def gates(q, h):
                hold(act, e["tv_ready"], q + 1, e["passed_a"])
                act.activation(ge[:, ds(h * TOPK, TOPK)], tv[:, :], ACT.Exp, bias=ntv[:, 0:1],
                               accum_out=gsum[:, ds(h, 1)]).then_inc(e["gate_done"], 1)

            def weights(n, ident, ahead=None):
                act.wait_ge(e["u_free"], U0 + TOPK * n + TOPK)
                act.activation(act_dots[:, :], dots[:, :], ACT.Gelu).then_inc(e["gelu_done"], 1)
                act.wait_ge(e["w_ready"], n + 1)
                for k in range(TOPK):
                    if k == ND and ahead is not None:
                        take_scores(*ahead)
                    act.wait_ge(e["v_free"], V0 + TOPK * n + k - ND + 1)
                    act.activation(diag[:, k % ND, :], ident[:, :], ACT.Copy, scale=wt[:, k:k + 1]).then_inc(e["diag_ready"], 1)

            def take_sums(t):
                act.wait_ge(e["y_turned"], 2 * t + 2)
                act.wait_ge(e["y_ready"], t + 1)
                for f in range(2):
                    last = act.activation(ysb[:, f * 512:(f + 1) * 512], yb[f][:, :], ACT.Copy)
                last.then_inc(e["y_copied"], 1)

            take_tokens(0)
            with act.Fori(0, PH) as h:
                take_scores(h, h)
                gates(h, h)
            take_scores(PH, 0)

            def tile(t, last):
                gates(PH * t + PH, 0)
                weights(PH * t, sh.ident, (PH * t + PH + 1, 1))
                act.wait_ge(e["advanced"], t + 1)
                take_tokens(t + 1)
                with act.Fori(1, PH - 1) as h:
                    gates(PH * t + PH + h, h)
                    weights(PH * t + h, sh.ident, (PH * t + PH + h + 1, h + 1))
                gates(PH * t + 2 * PH - 1, PH - 1)
                weights(PH * t + PH - 1, sh.ident, None if last else (PH * t + 2 * PH, 0))
                take_sums(t)
            with act.Fori(0, NT - 1) as t:
                tile(t, False)
            tile(NT - 1, True)
            act.wait_ge(e["fold_made"], 1)
            for hh in range(HS):
                weights(PH * NT + hh, fold)
            take_sums(NT)

        @block.vector
        def _(dve):
            st = Steps(dve, e["chain"])
            dve.wait_ge(e["fold_zeroed"], 1)
            for r in range(REP):
                last = dve.tensor_copy(fold[r * NS:(r + 1) * NS, 0:NS], sh.ident[r * NS:(r + 1) * NS, r * NS:(r + 1) * NS])
            last.then_inc(e["fold_made"], 1)
            dve.sem_inc(e["u_free"], U0)
            dve.wait_ge(e["iota_made"], 1)

            def pick(q, h):
                st.restart()
                hold(dve, e["gate_done"], q + 1, e["passed_v"])
                hold(dve, e["sc_copied"], q + 2, e["passed_v"])
                st.link(dve.tensor_copy(s1[:, :, :], sc[:, ds(2 * h, 2), :]))
                for lo, src in ((0, s1), (8, s2)):
                    for a in range(2):
                        st.did(dve.max(sv[:, a, lo:lo + 8], src[:, a, :]))
                    for a in range(2):
                        st.need(st.n - 1)
                        st.did(dve.max_index(si[:, a, lo:lo + 8], sv[:, a, lo:lo + 8], src[:, a, :]))
                    if lo == 0:
                        for a in range(2):
                            st.did(dve.match_replace(s2[:, a, :], sv[:, a, 0:8], s1[:, a, :], LOWEST))
                        st.need()
                st.need()
                st.link(dve.tensor_copy(sif[:, :, :], si[:, :, :]))
                st.did(dve.tensor_scalar(sbase[:, :], sif[:, 0, :], float(NK), None, ALU.mult))
                at, spans = 0, []
                for a0, a1, nb in blocks:
                    na = a1 - a0
                    spans.append((at, na, nb, a0, a1))
                    at += na * nb
                for dst, first, second in ((cand, sv[:, 0, :], sv[:, 1, :]), (cidx, sbase[:, :], sif[:, 1, :])):
                    if dst is cidx:
                        st.need(st.n - len(blocks))
                    for at, na, nb, a0, a1 in spans:
                        st.did(dve.tensor_tensor(dst[:, at:at + na * nb].rearrange("p (a b) -> p a b", b=nb),
                                                 first[:, a0:a1].unsqueeze(2).to_broadcast([P, na, nb]),
                                                 second[:, 0:nb].unsqueeze(1).to_broadcast([P, na, nb]), ALU.add))
                st.need(st.n - len(blocks))
                st.link(dve.max(tv[:, 0:8], cand[:, :]))
                st.did(dve.max_index(ti[:, 0:8], tv[:, 0:8], cand[:, :]))
                st.link(dve.match_replace(cand2[:, :], tv[:, 0:8], cand[:, :], LOWEST))
                st.link(dve.max(tv[:, 8:16], cand2[:, :]))
                st.did(dve.tensor_scalar(ntv[:, :], tv[:, 0:1], -1.0, None, ALU.mult))
                dve.max_index(ti[:, 8:16], tv[:, 8:16], cand2[:, :]).then_inc(e["tv_ready"], 1)
                hold(dve, e["tv_ready"], q + 1, e["passed_v"])
                st.link(dve.tensor_copy(tif[:, :], ti[:, :]))
                for k in range(TOPK):
                    st.did(dve.scalar_tensor_tensor(out=picked[:, k, :], in0=iota[:, :], scalar=tif[:, k:k + 1],
                                                    in1=cidx[:, :], op0=ALU.is_equal, op1=ALU.mult,
                                                    accum_out=ef[:, k:k + 1]))
                st.need()
                st.link(dve.tensor_copy(idx_next[:, ds(h * TOPK, TOPK)], ef[:, :]))

            def advance_indices(t, sample):
                if not (isinstance(t, int) and t == 0):
                    hold(dve, e["staged"], PH * t, e["passed_v"])
                if sample:
                    n = HS * TOPK
                    for r in range(REP):
                        last = dve.tensor_copy(idx_cur[r * NS:(r + 1) * NS, 0:n], idx_next[r * NS:(r + 1) * NS, r * n:(r + 1) * n])
                    last.then_inc(e["idx_ready"], 1)
                else:
                    dve.tensor_copy(idx_cur[:, :], idx_next[:, :]).then_inc(e["idx_ready"], 1)

            def advance(t, sample):
                if isinstance(t, int) and t == 0:
                    dve.wait_ge(e["xb_copied"], 2)
                    dve.wait_ge(e["gate_done"], PH + 1)
                else:
                    hold(dve, e["xb_copied"], 2 * t + 2, e["passed_v"])
                    hold(dve, e["gate_done"], PH * t + PH + 1, e["passed_v"])
                    hold(dve, e["u_free"], U0 + SLOTS * t, e["passed_v"])
                    hold(dve, e["w_ready"], PH * t, e["passed_v"])
                hold(dve, e["idx_ready"], t + 1, e["passed_v"])
                st.restart()
                st.link(dve.reciprocal(grec[:, :], gsum[:, :]))
                ge3 = ge[:, :].rearrange("p (h k) -> p h k", k=TOPK)
                gate3 = gate[:, :].rearrange("p (h k) -> p h k", k=TOPK)
                if sample:
                    for r in range(REP):
                        rows, hs = slice(r * NS, (r + 1) * NS), slice(r * HS, (r + 1) * HS)
                        st.did(dve.tensor_tensor(gate3[rows, 0:HS, :], ge3[rows, hs, :],
                                                 grec[rows, hs].unsqueeze(2).to_broadcast([NS, HS, TOPK]), ALU.mult))
                else:
                    st.did(dve.tensor_tensor(gate3, ge3, grec[:, :].unsqueeze(2).to_broadcast([P, PH, TOPK]), ALU.mult))
                dve.tensor_copy(xb[:, :], xbn[:, :]).then_inc(e["advanced"], 1)
                st.need()
                dve.wait_ge(e["advanced"], t + 1)

            def dot(n, col):
                for k in range(TOPK):
                    dve.wait_ge(u_in[k % NU], 16 * ((TOPK // NU) * n + k // NU + 1))
                    row = U[:, k % NU, :]
                    dve.tensor_tensor_reduce(out=row, in0=row, in1=xb[:, :], scale=1.0, scalar=0.0, op0=ALU.mult,
                                             op1=ALU.add, accum_out=dots[:, k:k + 1]).then_inc(e["u_free"], 1)
                hold(dve, e["gelu_done"], n + 2, e["passed_v"])
                hold(dve, e["diag_ready"], G0 + TOPK * n, e["passed_v"])
                dve.tensor_tensor(wt[:, :], gate[:, col], act_dots[:, :], ALU.mult).then_inc(e["w_ready"], 1)

            def add_sums(t, tok, n):
                for f in range(2):
                    hold(dve, e["y_turned"], 2 * t + f + 3, e["passed_v"])
                    h = sh.hT[:, 4 * f:4 * f + 4, tok]
                    dve.tensor_tensor(h, xt[f][:, :].rearrange("p (k n) -> p k n", n=P)[:, :, 0:n], h, ALU.add)\
                        .then_inc(e["y_added"], 1)

            with dve.Fori(0, PH) as h:
                pick(h, h)
            advance_indices(0, False)
            advance(0, False)
            pick(PH, 0)
            dot(0, slice(0, TOPK))

            def rest(t, sample):
                with dve.Fori(1, PH - 1) as h:
                    pick(PH * t + PH + h, h)
                    dot(PH * t + h, ds(h * TOPK, TOPK))
                pick(PH * t + 2 * PH - 1, PH - 1)
                advance_indices(t + 1, sample)
                dot(PH * t + PH - 1, slice(SLOTS - TOPK, SLOTS))
                advance(t + 1, sample)
            with dve.Fori(0, NT - 1) as t:
                rest(t, False)
                pick(PH * t + 2 * PH, 0)
                dot(PH * t + PH, slice(0, TOPK))
                add_sums(t, ds(t * P, P), P)
            rest(NT - 1, True)
            dot(PH * NT, slice(0, TOPK))
            add_sums(NT - 1, slice((NT - 1) * P, NT * P), P)
            for hh in range(1, HS):
                dot(PH * NT + hh, slice(hh * TOPK, (hh + 1) * TOPK))
            add_sums(NT, slice(SEQ, T), NS)


def load_ple(nc, sh, io, pT):
    PK = PLE // P
    with Scope(nc, "ple") as s:
        rows = s.sb("rows", [P, NT + 1, PLE])
        banks = [s.ps(f"b{k}{i}") for k in range(PK) for i in range(3)]
        loaded, turned = s.sem("loaded"), s.sem("turned")
        block = s.block()

        @block.sync
        def _(sp):
            sp.dma_start(rows[:, 0:NT, :], io["p_prompt"][0, 0].rearrange("(t p) d -> p t d", p=P)).then_inc(loaded, 16)
            sp.dma_start(rows[0:NS, NT, :], io["p_sample"][0].rearrange("b s d -> (b s) d")).then_inc(loaded, 16)

        @block.tensor
        def _(pe):
            pe.wait_ge(loaded, 32)
            for k in range(PK):
                for t in range(NT + 1):
                    n = P if t < NT else NS
                    last = pe.transpose(banks[3 * k + t // 4][:, (t % 4) * P:(t % 4) * P + n],
                                        rows[0:n, t, k * P:(k + 1) * P], sh.ident[0:n, 0:n])
            last.then_inc(turned, 1)

        @block.vector
        def _(dve):
            dve.wait_ge(turned, 1)
            for k in range(PK):
                for i in range(3):
                    lo, hi = i * 512, min(T, i * 512 + 512)
                    dve.tensor_copy(pT[:, k, lo:hi], banks[3 * k + i][:, 0:hi - lo])


def add_ple(nc, sh, io, uT, u_at, pT, p_at):
    wg, wp = w_view(io["w_ple_gate"]), w_view(io["w_ple"])
    PK = PLE // P
    with Scope(nc, "gate") as s:
        pr = SplitProduct(nc, s, KD // 2, lambda i, j: (wg, wp)[j % 2][:, :, ds((2 * i + j // 2) * P, P)], [KD, PK] * 2,
                          lambda j, k, c: pr.parts_of(j % 2, k, c), [(uT, u_at), (pT, p_at)])
        sg = s.sb("sg", [P, 2, T])
        tmp = s.sb("tmp", [P, 2, T])
        passed_v, used, made, added = (s.sem(x) for x in ("passed_v", "sig_used", "made", "added"))
        block = s.block()
        block.sync(pr.load)
        block.tensor(pr.multiply)
        block.gpsimd(pr.split_weights)

        @block.scalar
        def _(act):
            pr.x_highs(act)
            act.sem_inc(used, 2)
            with act.Fori(0, KD // 2) as i:
                for j in (0, 2):
                    act.wait_ge(used, 2 * i + j // 2 + 1)
                    for c in range(NCH):
                        act.wait_ge(pr.ready, pr.ready_at(i, j, c))
                        pr.frees(j, act.activation(sg[:, j // 2, cols(c)], pr.bank(j, c), ACT.Sigmoid))

        @block.vector
        def _(dve):
            pr.x_lows(dve)
            dve.sem_inc(added, 1)
            with dve.Fori(0, KD // 2) as i:
                for j in (1, 3):
                    hold(dve, added, 2 * i + j // 2 + 1, passed_v)
                    for c in range(NCH):
                        hold(dve, pr.free[0], NCH * (2 * i + j // 2) + NCH + c + 1, passed_v)
                        hold(dve, pr.ready, pr.ready_at(i, j, c), passed_v)
                        pr.frees(j, dve.tensor_tensor(tmp[:, j // 2, cols(c)], pr.bank(j, c), sg[:, j // 2, cols(c)], ALU.mult))
                    hold(dve, pr.free[1], NCH * (2 * i + j // 2) + 2 * NCH, passed_v)
                    dve.sem_inc(used, 1)
                    h = flat(sh.hT[:, ds(2 * i + j // 2, 1), :])
                    dve.tensor_tensor(h, tmp[:, j // 2, :], h, ALU.add).then_inc(added, 1)


def store_tokens(nc, sh, io, yT):
    with Scope(nc, "store") as s:
        out = s.sb("out", [P, NT + 1, D])
        banks = [[s.ps(f"b{b}{h}") for h in range(2)] for b in range(2)]
        turned = [s.sem("low_turned"), s.sem("high_turned")]
        copied = [s.sem("act_copied"), s.sem("dve_copied")]
        stored = s.sem("stored")
        block = s.block()

        @block.tensor
        def _(pe):
            for t in range(NT + 1):
                n = P if t < NT else NS
                for h in range(2):
                    if t >= 2:
                        pe.wait_ge(copied[h], t - 1)
                    for k in range(4):
                        last = pe.transpose(banks[t % 2][h][0:n, k * P:(k + 1) * P], yT[:, 4 * h + k, t * P:t * P + n], sh.ident[:, :])
                    last.then_inc(turned[h], 1)

        def copy_out(eng, h, copy):
            for t in range(NT + 1):
                n = P if t < NT else NS
                eng.wait_ge(turned[h], t + 1)
                copy(out[0:n, t, h * 512:(h + 1) * 512], banks[t % 2][h][0:n, :]).then_inc(copied[h], 1)

        @block.scalar
        def _(act):
            copy_out(act, 0, lambda o, i: act.activation(o, i, ACT.Copy))

        @block.vector
        def _(dve):
            copy_out(dve, 1, dve.tensor_copy)

        @block.sync
        def _(sp):
            yp = io["y_prompt"][0].rearrange("(t p) d -> t p d", p=P)
            for t in range(NT + 1):
                sp.wait_ge(copied[0], t + 1)
                sp.wait_ge(copied[1], t + 1)
                if t < NT:
                    sp.dma_start(yp[t], out[:, t, :]).then_inc(stored, 16)
                else:
                    sp.dma_start(io["y_sample"].rearrange("b s d -> (b s) d"), out[0:NS, NT, :]).then_inc(stored, 16)
            sp.wait_ge(stored, 16 * (NT + 1))


def program(nc, io):
    with Scope(nc, "all") as s:
        sh = Shared()
        sh.ident, sh.ones, sh.zeros = s.sb("ident", [P, P]), s.sb("ones", [P, P]), s.sb("zeros", [P, 512])
        sh.vec, sh.wdw, sh.bf = s.sb("vec", [P, NVEC]), s.sb("wdw", [P, CWID * CK]), s.sb("bf", [H, 1])
        sh.hT = s.sb("hT", [P, KD, T])
        sh.q_s = nc.dram_tensor("q_rows", (H, DH + 2, SEQ), F32, kind="Internal").ap()
        sh.k_s = nc.dram_tensor("k_rows", (H, DH + 2, SEQ), F32, kind="Internal").ap()
        sh.cum_s = nc.dram_tensor("cum_rows", (2, NG, H, GRP * SD), F32, kind="Internal").ap()
        sh.ex_s = nc.dram_tensor("decay_rows", (NG, P, H, PAGE), F32, kind="Internal").ap()
        sh.m_s = nc.dram_tensor("mixed_rows", (P, KD, T), F32, kind="Internal").ap()
        sh.u_s = nc.dram_tensor("token_tiles", (NT + 1, P, KD, P), F32, kind="Internal").ap()
        sh.lf_gathered = [s.sem(f"lf_gathered{g}") for g in range(NG)]
        sh.pages_loaded = [[s.sem(f"pages_loaded{g}_{b}") for b in range(GRP // 2)] for g in range(NG)]
        sh.tokens_stored = s.sem("tokens_stored")
        sh.u_loaded = [s.sem(f"u_loaded{i}") for i in range(8)]
        sh.v_loaded = [s.sem(f"v_loaded{i}") for i in range(8)]
        load_tokens(nc, sh, io)
        with Scope(nc, "mix") as m:
            uT, u_at = m.placed("uT", [P, KD, T])
            attT = m.sb("attT", [P, AC, T])
            rms_norm(nc, sh, "norm1", sh.hT, V_MIX, uT)
            with Scope(nc, "heads") as hd:
                qkvS = hd.sb("qkvS", [P, 3 * AC, NS])
                with Scope(nc, "v") as v:
                    vtok, v_at = v.placed("vtok", [P, NT + 1, AW])
                    with Scope(nc, "qkv") as q:
                        qkvT = q.sb("qkvT", [P, 3 * AC, T])
                        project_qkv(nc, sh, io, uT, u_at, qkvT, attT, v_at)
                        heads_prepare(nc, sh, io, uT, qkvT, qkvS, vtok)
                    prompt_attention(nc, sh, io, vtok, attT)
                yT = hd.sb("yT", [P, CK, T])
                with Scope(nc, "convin") as c:
                    gp, gs = c.sb("gp", [P, CK, PAD + SEQ]), c.sb("gs", [P, CK, BD, PAD + SD])
                    taps = conv_taps(sh, [c.sem(f"conv_done{k}") for k in range(2 * CK)], gp, gs, yT)
                    glu_inputs(nc, sh, io, uT, u_at, gp, gs, yT)
                    cache_decay(nc, sh, io)
                    in_group = [TAPS_K * NTURN + v * NTURN // 2 for v in TAPS_V]
                    early = CWID - sum(in_group)
                    sample_attention(nc, sh, io, 0, qkvS, attT, taps, 0, early, TAPS_K, TAPS_V[0])
                    done = early + in_group[0]
                    sample_attention(nc, sh, io, 1, qkvS, attT, taps, done, done, TAPS_K, TAPS_V[1])
                conv_norm(nc, sh, yT)
                merge(nc, sh, io, uT, u_at, attT, yT)
            residual_product(nc, sh, "out", io["w_out"], uT, u_at)
        with Scope(nc, "ffn") as m:
            wk = m.sb("wk", [P, KD, 2 * PH, P])
            with Scope(nc, "tokens") as q:
                uT = q.sb("u2T", [P, KD, T])
                rms_norm(nc, sh, "norm2", sh.hT, V_FFN, uT)
                key_weights(nc, sh, io, uT, wk)
            experts(nc, sh, io, wk)
        with Scope(nc, "last") as m:
            uT, u_at = m.placed("u3T", [P, KD, T])
            pT, p_at = m.placed("pT", [P, PLE // P, T])
            load_ple(nc, sh, io, pT)
            rms_norm(nc, sh, "norm3", sh.hT, V_PLE, uT)
            add_ple(nc, sh, io, uT, u_at, pT, p_at)
            rms_norm(nc, sh, "norm4", sh.hT, V_FIN, uT)
            store_tokens(nc, sh, io, uT)


_INS = ["x_prompt", "x_sample", "cache_k", "cache_v", "cache_lf", "state_conv", "page_table", "p_prompt", "p_sample",
        "g_mix", "w_in", "b_f", "w_dw", "b_dw", "ln_g", "ln_b", "w_conv_proj", "w_att_proj", "w_out", "g_ffn", "w_pq",
        "sub_keys", "exp_u", "exp_v", "g_ple", "w_ple", "w_ple_gate", "g_final"]
_OUTS = [("y_prompt", (1, SEQ, D)), ("y_sample", (BD, SD, D)), ("k_prompt", (1, 1, SEQ, H, DH)),
         ("v_prompt", (1, 1, SEQ, H, DH)), ("lf_prompt", (1, 1, SEQ, H)), ("conv_prompt", (1, 1, PAD, CC)),
         ("k_sample", (1, BD, SD, H, DH)), ("v_sample", (1, BD, SD, H, DH)), ("lf_sample", (1, BD, SD, H)),
         ("conv_sample", (1, BD, PAD, CC))]


def kernel(**inputs):
    import numpy as _np
    import concourse.bacc as _bacc
    from concourse import mybir as _mybir
    from concourse.bass_utils import run_bass_kernel_spmd as _run

    nc = _bacc.Bacc("TRN2", target_bir_lowering=False, num_devices=1)
    arrays, tensors = {}, {}
    for name in _INS:
        a = _np.ascontiguousarray(inputs[name])
        arrays[f"in_{name}"] = a
        tensors[name] = nc.dram_tensor(f"in_{name}", a.shape, _mybir.dt.from_np(a.dtype), kind="ExternalInput").ap()
    for name, shape in _OUTS:
        tensors[name] = nc.dram_tensor(f"out_{name}", shape, _mybir.dt.float32, kind="ExternalOutput").ap()
    program(nc, tensors)
    r = _run(nc, [arrays], core_ids=[0])
    return tuple(r.results[0][f"out_{name}"] for name, _ in _OUTS)
```
